# Optimizing a Trainium2 kernel written in Bass

```python
import math
import jax, jax.numpy as jnp
from jax import lax
import numpy as np

D_MODEL = 1024
BATCH = 1
SEQ = 256
DEPTH = 2
DEC_BATCH = 8
DEC_SEQ = 4
PAST_LEN = 1024
PAGE_SIZE = 128

HEAD_DIM = 64
MIX_W = D_MODEL
N_HEADS = MIX_W // HEAD_DIM
GLA_HEADS = N_HEADS // 4
GM_HEADS = N_HEADS // 4
SB_HEADS = N_HEADS - GLA_HEADS - GM_HEADS
GLA_W = GLA_HEADS * HEAD_DIM
GM_W = GM_HEADS * HEAD_DIM
SB_W = SB_HEADS * HEAD_DIM
GLA_LOWRANK = 16
GLA_TAU = 16.0
GLA_CHUNK = 64
GM_CHUNK = 128
SB_BLOCK = 128
SB_BIAS_INIT = -6.0
D_FF = ((8 * D_MODEL // 3 + 127) // 128) * 128
N_COND = 9
MACARON_W = 0.5
EPS = 1e-6
IN_COLS = 4 * GLA_W + GLA_LOWRANK + 2 * GM_W + 3 * SB_W

kernel_name = "hymba_gla_gmlp_stickbreak_macaron_decode"

def rmsnorm(x, w):
    xf = x.astype(jnp.float32)
    y = xf * lax.rsqrt(jnp.mean(xf * xf, axis=-1, keepdims=True) + EPS)
    return (y * w.astype(jnp.float32)).astype(x.dtype)

def swiglu(a, w_in, w_out):
    g, u = jnp.split(a @ w_in, 2, axis=-1)
    return (jax.nn.silu(g) * u) @ w_out

def split_cols(h):
    sizes = [GLA_W, GLA_W, GLA_W, GLA_W, GLA_LOWRANK, GM_W, GM_W, SB_W, SB_W, SB_W]
    idx, acc = [], 0
    for s in sizes[:-1]:
        acc += s
        idx.append(acc)
    return jnp.split(h, idx, axis=-1)

def gla_chunked(q, k, v, log_a, s0):
    B, L, H, DK = q.shape
    C = GLA_CHUNK if L % GLA_CHUNK == 0 else L
    n = L // C

    def to_chunks(t):
        return t.astype(jnp.float32).reshape(B, n, C, H, t.shape[-1]).transpose(1, 0, 3, 2, 4)

    qc, kc, vc, ac = (to_chunks(q * (DK ** -0.5)), to_chunks(k), to_chunks(v), to_chunks(log_a))
    causal = jnp.tril(jnp.ones((C, C), dtype=bool))

    def step(S, inp):
        qi, ki, vi, ai = inp
        b = jnp.cumsum(ai, axis=-2)
        q_t = qi * jnp.exp(b)
        k_t = ki * jnp.exp(-b)
        att = jnp.where(causal, jnp.einsum('bhtk,bhsk->bhts', q_t, k_t), 0.0)
        o = jnp.einsum('bhtk,bhkv->bhtv', q_t, S) + jnp.einsum('bhts,bhsv->bhtv', att, vi)
        b_last = b[:, :, -1:, :]
        k_end = ki * jnp.exp(b_last - b)
        S_new = S * jnp.exp(b_last[:, :, 0, :, None]) + jnp.einsum('bhsk,bhsv->bhkv', k_end, vi)
        return S_new, o

    S, o = lax.scan(step, s0.astype(jnp.float32), (qc, kc, vc, ac))
    o = o.transpose(1, 0, 3, 2, 4).reshape(B, L, H, v.shape[-1])
    return o, S

def gla_mixer(q, k, v, g, lr, w_gate2, b_gate, norm_w, s0):
    B, L, _ = q.shape
    log_a = jax.nn.log_sigmoid((lr @ w_gate2 + b_gate).astype(jnp.float32)) / GLA_TAU
    hs = lambda t: t.reshape(B, L, GLA_HEADS, HEAD_DIM)
    o, S = gla_chunked(hs(q), hs(k), hs(v), hs(log_a), s0)
    o = rmsnorm(o.astype(q.dtype), norm_w.reshape(GLA_HEADS, HEAD_DIM))
    return o.reshape(B, L, GLA_W) * jax.nn.silu(g), S

def gmlp_mixer(u, v, ln_w, ln_b, w_s, b_s):
    B, L, _ = v.shape
    vf = v.astype(jnp.float32)
    mu = jnp.mean(vf, axis=-1, keepdims=True)
    var = jnp.mean((vf - mu) ** 2, axis=-1, keepdims=True)
    vn = ((vf - mu) * lax.rsqrt(var + EPS) * ln_w.astype(jnp.float32)
          + ln_b.astype(jnp.float32)).astype(v.dtype)
    n = -(-L // GM_CHUNK)
    pad = n * GM_CHUNK - L
    vp = jnp.pad(vn, ((0, 0), (0, pad), (0, 0))).reshape(B, n, GM_CHUNK, GM_HEADS, HEAD_DIM)
    w = jnp.where(jnp.tril(jnp.ones((GM_CHUNK, GM_CHUNK), dtype=bool)), w_s, 0.0)
    s = jnp.einsum('hts,bnshd->bnthd', w, vp) + b_s.T[None, None, :, :, None]
    s = s.reshape(B, n * GM_CHUNK, GM_W)[:, :L]
    return u * s, vn

def sb_block(q, k, v, q_pos, bias):
    z = (jnp.einsum('bthd,bshd->bhts', q, k).astype(jnp.float32) * (HEAD_DIM ** -0.5)
         + bias.astype(jnp.float32)[None, :, None, None])
    kpos = jnp.arange(k.shape[1])
    mask = kpos[None, :] < q_pos[:, None]
    log1m = jnp.where(mask, -jax.nn.softplus(z), 0.0)
    suffix = lax.cumsum(log1m, axis=3, reverse=True) - log1m
    A = jnp.where(mask, jnp.exp(jax.nn.log_sigmoid(z) + suffix), 0.0)
    return jnp.einsum('bhts,bshd->bthd', A.astype(v.dtype), v)

def sb_attend(q, k, v, pos0, bias):
    T = q.shape[1]
    outs = []
    for start in range(0, T, SB_BLOCK):
        end = min(start + SB_BLOCK, T)
        kl = pos0 + end
        outs.append(sb_block(q[:, start:end], k[:, :kl], v[:, :kl],
                             pos0 + jnp.arange(start, end), bias))
    return jnp.concatenate(outs, axis=1)

def gather_pages(cache, page_table):
    g = cache[page_table]
    return g.reshape(page_table.shape[0], -1, SB_HEADS, HEAD_DIM)

def mixer(a, w_in, w_out, gla_w2, gla_b, gla_nw, gm_ln_w, gm_ln_b, gm_ws, gm_bs, sb_b,
          gla_s0, past_k, past_v):
    B, L, _ = a.shape
    gq, gk, gv, gg, glr, mu, mv, sq, sk, sv = split_cols(a @ w_in)
    o_gla, s_gla = gla_mixer(gq, gk, gv, gg, glr, gla_w2, gla_b, gla_nw, gla_s0)
    o_gm, v_gm = gmlp_mixer(mu, mv, gm_ln_w, gm_ln_b, gm_ws, gm_bs)
    hs = lambda t: t.reshape(B, L, SB_HEADS, HEAD_DIM)
    k_new, v_new = hs(sk), hs(sv)
    if past_k is None:
        kk, vv, pos0 = k_new, v_new, 0
    else:
        kk = jnp.concatenate([past_k.astype(k_new.dtype), k_new], axis=1)
        vv = jnp.concatenate([past_v.astype(v_new.dtype), v_new], axis=1)
        pos0 = past_k.shape[1]
    o_sb = sb_attend(hs(sq), kk, vv, pos0, sb_b).reshape(B, L, SB_W)
    o = jnp.concatenate([o_gla, o_gm, o_sb], axis=-1) @ w_out
    return o, s_gla, v_gm, k_new, v_new

def decoder_layer(x, c, cond_w, cond_b, norm_pre, norm_post, ffn_w_in, ffn_w_out, mix_w_in,
                  mix_w_out, gla_w2, gla_b, gla_nw, gm_ln_w, gm_ln_b, gm_ws, gm_bs, sb_b,
                  gla_s0, past_k, past_v):
    m = (jax.nn.silu(c) @ cond_w + cond_b).reshape(c.shape[0], N_COND, 1, D_MODEL)

    def pre(i, h):
        return rmsnorm(h, norm_pre[i]) * (1.0 + m[:, 3 * i + 1]) + m[:, 3 * i]

    def post(i, h, y, rw):
        return h + rw * m[:, 3 * i + 2] * rmsnorm(y, norm_post[i])

    x = post(0, x, swiglu(pre(0, x), ffn_w_in[0], ffn_w_out[0]), MACARON_W)
    o, s_gla, v_gm, k_new, v_new = mixer(pre(1, x), mix_w_in, mix_w_out, gla_w2, gla_b, gla_nw,
                                         gm_ln_w, gm_ln_b, gm_ws, gm_bs, sb_b, gla_s0,
                                         past_k, past_v)
    x = post(1, x, o, 1.0)
    x = post(2, x, swiglu(pre(2, x), ffn_w_in[1], ffn_w_out[1]), MACARON_W)
    return x, s_gla, v_gm, k_new, v_new

def setup_inputs(seed: int = 0) -> dict:
    key = jax.random.key(seed)
    ks = jax.random.split(key, 26)
    f32 = jnp.float32
    nrm = lambda k, shape, s: jax.random.normal(k, shape, f32) * s
    n_pages = PAST_LEN // PAGE_SIZE
    n_used = DEC_BATCH * n_pages
    n_pool = n_used + max(1, n_used // 4)
    perm = jax.random.permutation(ks[0], n_pool)
    page_table = perm[:n_used].reshape(DEC_BATCH, n_pages).astype(jnp.int32)
    return {
        "x_prompt": nrm(ks[1], (BATCH, SEQ, D_MODEL), 1.0),
        "x_sample": nrm(ks[2], (DEC_BATCH, DEC_SEQ, D_MODEL), 1.0),
        "c_prompt": nrm(ks[3], (BATCH, D_MODEL), 1.0),
        "c_sample": nrm(ks[4], (DEC_BATCH, D_MODEL), 1.0),
        "cache_sb_k": nrm(ks[5], (DEPTH, n_pool, PAGE_SIZE, SB_HEADS, HEAD_DIM), 1.0),
        "cache_sb_v": nrm(ks[6], (DEPTH, n_pool, PAGE_SIZE, SB_HEADS, HEAD_DIM), 1.0),
        "state_gla": nrm(ks[7], (DEPTH, DEC_BATCH, GLA_HEADS, HEAD_DIM, HEAD_DIM), 1.0),
        "page_table": page_table,
        "cond_w": nrm(ks[8], (DEPTH, D_MODEL, N_COND * D_MODEL), 0.5 * D_MODEL ** -0.5),
        "cond_b": nrm(ks[9], (DEPTH, N_COND * D_MODEL), 0.02),
        "norm_pre": 1.0 + nrm(ks[10], (DEPTH, 3, D_MODEL), 0.05),
        "norm_post": 1.0 + nrm(ks[11], (DEPTH, 3, D_MODEL), 0.05),
        "ffn_w_in": nrm(ks[12], (DEPTH, 2, D_MODEL, 2 * D_FF), D_MODEL ** -0.5),
        "ffn_w_out": nrm(ks[13], (DEPTH, 2, D_FF, D_MODEL), D_FF ** -0.5),
        "mix_w_in": nrm(ks[14], (DEPTH, D_MODEL, IN_COLS), D_MODEL ** -0.5),
        "mix_w_out": nrm(ks[15], (DEPTH, MIX_W, D_MODEL), MIX_W ** -0.5),
        "gla_w_gate2": nrm(ks[16], (DEPTH, GLA_LOWRANK, GLA_W), GLA_LOWRANK ** -0.5),
        "gla_b_gate": nrm(ks[17], (DEPTH, GLA_W), 0.1),
        "gla_norm": 1.0 + nrm(ks[18], (DEPTH, GLA_W), 0.05),
        "gm_ln_w": 1.0 + nrm(ks[19], (DEPTH, GM_W), 0.05),
        "gm_ln_b": nrm(ks[20], (DEPTH, GM_W), 0.02),
        "gm_ws": nrm(ks[21], (DEPTH, GM_HEADS, GM_CHUNK, GM_CHUNK), GM_CHUNK ** -0.5),
        "gm_bs": 1.0 + nrm(ks[22], (DEPTH, GM_HEADS, GM_CHUNK), 0.1),
        "sb_bias": SB_BIAS_INIT + nrm(ks[23], (DEPTH, SB_HEADS), 0.5),
    }

def reference(x_prompt, x_sample, c_prompt, c_sample, cache_sb_k, cache_sb_v, state_gla,
              page_table, cond_w, cond_b, norm_pre, norm_post, ffn_w_in, ffn_w_out, mix_w_in,
              mix_w_out, gla_w_gate2, gla_b_gate, gla_norm, gm_ln_w, gm_ln_b, gm_ws, gm_bs,
              sb_bias):
    xp, xs = x_prompt, x_sample
    gla_p, gla_s, kp, vp, ksl, vsl, gms = [], [], [], [], [], [], []
    s0_prompt = jnp.zeros((x_prompt.shape[0], GLA_HEADS, HEAD_DIM, HEAD_DIM), jnp.float32)
    for l in range(DEPTH):
        w = (cond_w[l], cond_b[l], norm_pre[l], norm_post[l], ffn_w_in[l], ffn_w_out[l],
             mix_w_in[l], mix_w_out[l], gla_w_gate2[l], gla_b_gate[l], gla_norm[l],
             gm_ln_w[l], gm_ln_b[l], gm_ws[l], gm_bs[l], sb_bias[l])
        xp, sg, _, k_new, v_new = decoder_layer(xp, c_prompt, *w, s0_prompt, None, None)
        gla_p.append(sg)
        kp.append(k_new)
        vp.append(v_new)
        past_k = gather_pages(cache_sb_k[l], page_table)
        past_v = gather_pages(cache_sb_v[l], page_table)
        xs, sg2, gv, k2, v2 = decoder_layer(xs, c_sample, *w, state_gla[l], past_k, past_v)
        gla_s.append(sg2)
        ksl.append(k2)
        vsl.append(v2)
        gms.append(gv)
    return (xp, xs, jnp.stack(gla_p), jnp.stack(gla_s), jnp.stack(kp), jnp.stack(vp),
            jnp.stack(ksl), jnp.stack(vsl), jnp.stack(gms))


_drawn_inputs = setup_inputs


def setup_inputs(seed=0):
    import zlib

    import numpy as np

    out = dict(_drawn_inputs(seed))
    spreads = {}
    factors = {'gla_norm': 17.945,
     'gm_ln_b': 2.938,
     'sb_bias': 38.304,
     'cache_sb_k': 8.0,
     'cache_sb_v': 8.0,
     'gm_bs': 4.346}
    for name, (base, spread) in spreads.items():
        noise = np.random.default_rng([zlib.crc32(name.encode()), seed]).standard_normal(out[name].shape)
        drawn = base * np.exp(spread * noise) if base else spread * noise
        out[name] = __import__('jax').numpy.asarray(drawn.astype(out[name].dtype))
    for name, factor in factors.items():
        out[name] = (out[name] * factor).astype(out[name].dtype)
    return out
```

```python
from contextlib import ExitStack

import numpy as np
import concourse.bass as bass
from concourse import mybir

F32 = mybir.dt.float32
F32R = mybir.dt.float32r
I32 = mybir.dt.int32
ALU = mybir.AluOpType
ACT = mybir.ActivationFunctionType
ds = bass.ds

P = 128
EPS = 1e-6
MASKED = -1e30
SOFTPLUS_TABLES = "natural_log_exp_and_others"


class Signal:

    def __init__(self, sem, per_layer, start=0):
        self.sem, self.per_layer, self.start = sem, per_layer, start

    def at(self, layer, k):
        return layer * self.per_layer + (self.start + k)


def decoder_step(nc, x_prompt, x_sample, c_prompt, c_sample, cache_sb_k, cache_sb_v, state_gla,
                 page_table, cond_w, cond_b, norm_pre, norm_post, ffn_w_in, ffn_w_out, mix_w_in,
                 mix_w_out, gla_w_gate2, gla_b_gate, gla_norm, gm_ln_w, gm_ln_b, gm_ws, gm_bs,
                 sb_bias, y_prompt, y_sample, s_prompt, s_sample, k_prompt, v_prompt, k_sample,
                 v_sample, gm_v_sample):
    L, NPOOL, PAGE, SBH, HD = cache_sb_k.shape
    D = x_prompt.shape[2]
    NP = x_prompt.shape[1]
    B, TS = x_sample.shape[:2]
    NS = B * TS
    T = NP + NS
    KB = D // P
    FF = ffn_w_out.shape[2]
    FB = FF // P
    NC = 1 + B
    NPG = page_table.shape[1]
    GH = state_gla.shape[2]
    GW = GH * HD
    SBW = SBH * HD
    LR = gla_w_gate2.shape[1]
    TAU = 16.0
    GC = 64
    CPB = NP // GC
    PT_ = NP // P
    PR = SBH // 2
    GP = GH // 2
    assert (D, NP, NS, FB, NPG, PAGE, PR, GP, PT_) == (1024, 256, 32, 22, 8, 128, 4, 2, 2)

    GQ, GK, GV, GG, MU, MV, SK, SQ, SV = 0, 2, 4, 6, 8, 10, 12, 16, 20
    NF = 24
    LRC = 4 * GW

    N_IN, N_OUT, N_MI, N_MO = FB, 2 * KB, NF // 2, KB // 2
    POS_IN = [0, N_IN + N_OUT + N_MI + N_MO]
    POS_OUT = [N_IN, POS_IN[1] + N_IN]
    POS_MI = N_IN + N_OUT
    POS_MO = POS_MI + N_MI
    NW = POS_OUT[1] + N_OUT
    NCH = 3 * D // 256
    NPC = B * NPG // 4
    DP_C = [2 * NCH + 2 * NPC, 0, NCH]
    DP_K = 2 * NCH
    DP_V = DP_K + NPC
    ND = 3 * NCH + 2 * NPC
    YB_OUT = [0, KB + 2 + N_MO + 2]
    YB_MO = KB + 2

    ctx = ExitStack()
    with ctx:
        sems = []

        def signal(name, per_layer=1, start=0):
            s = Signal(ctx.enter_context(nc.semaphore(name)), per_layer, start)
            sems.append(s)
            return s

        BASE = 16512
        TOP = 229344
        at = [BASE]

        def tile(name, shape, dt=F32, offset=None):
            words = int(np.prod(shape[1:]))
            here = at[0] if offset is None else offset
            t = nc.alloc_sbuf_tensor_at(name, shape, dt, offset=here)
            if offset is None:
                at[0] += -(-words * 4 // 32) * 32
            assert here + words * 4 <= TOP, (name, here, words)
            return t

        raw = tile("raw", [P, 2, 2048])
        w_hi = tile("w_hi", [P, 2, 2048], F32R)
        w_lo = tile("w_lo", [P, 2, 2048], F32R)
        direct = tile("direct", [P, 4, 2048])
        X = tile("X", [P, KB, T])
        y_region = at[0]
        Y = tile("Y", [P, KB, T])
        a_region = at[0]
        a_hi = tile("a_hi", [P, KB, T], F32R)
        a_lo = tile("a_lo", [P, KB, T], F32R)
        a_end = at[0]
        M = tile("M", [P, 3, NF, NC])
        cT = tile("cT", [P, KB, 32])
        crow = tile("crow", [P, NCH // 2 * P])
        vecs = tile("vecs", [P, L, P])
        vec = tile("vec", [P, P])
        V_CB, V_PRE, V_POST, V_GB, V_GN, V_LW, V_LB = 0, 72, 96, 120, 122, 124, 126
        std = tile("std", [P, T])
        rstd = tile("rstd", [P, T])
        ident = tile("ident", [P, P])
        ones = tile("ones", [P, P])
        head_ones = tile("head_ones", [P, P])
        suffix = tile("suffix", [P, P])
        causal = tile("causal", [P, P])
        gla_mask = tile("gla_mask", [P, P])
        neg_mask = tile("neg_mask", [P, P])
        gla_mask_s = tile("gla_mask_s", [NS, NS])
        neg_mask_s = tile("neg_mask_s", [NS, NS])
        same_s = tile("same_s", [NS, B])
        rep = tile("rep", [TS, B, TS])
        restart = tile("restart", [P, T])
        pages = tile("pages", [1, B * NPG], I32)
        w2 = tile("w2", [LR, GW])
        sbb = tile("sbb", [P, SBH])
        lr = tile("lr", [LR, T])
        eps = tile("eps", [P, 1])
        shared = at[0]

        h_hi = tile("h_hi", [P, FB, T], F32R, shared)
        h_lo = tile("h_lo", [P, FB, T], F32R, shared + FB * T * 4)
        sg = tile("sg", [P, 2, T], F32, shared + 2 * FB * T * 4)
        hf = tile("hf", [P, 2, T], F32, shared + 2 * FB * T * 4 + 2 * T * 4)
        ysq = tile("ysq", [P, 4, T], F32, shared + 2 * FB * T * 4)
        xsq = tile("xsq", [P, KB, T], F32, shared)
        xtok = tile("xtok", [P, 3, D], F32, shared)
        ctok = tile("ctok", [NC, D], F32, shared + 3 * D * 4)
        vrow = tile("vrow", [P, L, P], F32, shared + 4 * D * 4)
        at[0] = shared
        Fm = tile("Fm", [P, NF, T])
        qz = tile("qz", [P, PR, 2, T])
        sv = tile("sv", [P, 3, SBW])
        g0 = at[0]
        gt = [tile(f"gt{i}", [P, GP, T]) for i in range(4)]
        gqz = tile("gqz", [P, GP, 2, T])
        gv = tile("gv", [P, 3, GW])
        kend = tile("kend", [P, CPB + 1, GW])
        att = tile("att", [P, PT_, GP, 2, P])
        att_s = tile("att_s", [NS, GP, 2, NS])
        S = tile("S", [P, 2, GP, P])
        S0 = tile("S0", [P, B, GP, HD])
        lr_raw = tile("lr_raw", [P, KB, LR], F32, g0 + 4 * 4 * GP * T - 4 * GP * T)
        assert at[0] <= TOP, at[0] - TOP
        lrw_hi = tile("lrw_hi", [P, KB, P], F32R, g0 + 4 * 4 * GP * T)
        lrw_lo = tile("lrw_lo", [P, KB, P], F32R, g0 + 4 * 4 * GP * T + KB * P * 4)
        NZ = B * NPG * SBH * TS
        z = tile("z", [P, NZ + SBH * NS], F32, shared + SQ * T * 4)
        at[0] = g0
        sm = tile("sm", [P, NZ + SBH * NS])
        sn = tile("sn", [P, NZ + SBH * NS])
        a_st = tile("a_st", [P, 2, NPG * 8 * TS])
        an_st = tile("an_st", [NS, SBH, 2 * TS])
        assert at[0] <= TOP, at[0] - TOP
        at[0] = a_region
        kst = tile("kst", [P, 3, SBW], F32, y_region)
        kt = tile("kt", [P, 2, 512])
        qd = tile("qd", [P, PR, 2, 2 * TS])
        vm = tile("vm", [NS, B, P], F32, at[0])
        dm = tile("dm", [P, GP, T])
        dsq = tile("dsq", [P, GP, T])
        vn = tile("vn", [P, 3, GW])
        wsr = tile("wsr", [P, GH, P])
        wst = tile("wst", [P, GH, P])
        wss = tile("wss", [NS, GH, NS])
        bs = tile("bs", [P, GP, P])
        assert at[0] <= a_end, at[0] - a_end
        zp0 = tile("zp0", [P, SBH, NP], F32, a_region)
        zp1 = tile("zp1", [P, SBH, P], F32, a_region + SBH * NP * 4)

        PS = ctx.enter_context(nc.psum_tensor("PS", [P, 8, 512], F32))

        raw_in = [[signal(f"raw_in{s}{h}", NW // 2) for h in range(2)] for s in range(2)]
        direct_in = [signal(f"direct_in{s}", ND // 4, NCH // 4) for s in range(4)]
        hi_done = signal("hi_done", 2 * NW)
        lo_done = signal("lo_done", 2 * NW, 4)
        w_used = signal("w_used", NW, 2)
        direct_used = signal("direct_used", ND, 4 + NCH)
        rows_in = signal("rows_in")
        small_in = signal("small_in")
        ws_in = signal("ws_in")
        s0_in = signal("s0_in")
        bs_in = signal("bs_in")
        const_ready = signal("const_ready")
        tposed = signal("tposed")
        start_copied = signal("start_copied")
        c_silu = signal("c_silu")
        cond_copied = signal("cond_copied", 3 * NCH // 2, 2 + NCH // 2)
        cond_t = signal("cond_t", 3, 1)
        mod_ready = signal("mod_ready", 3, 1)
        gu_free = signal("gu_free", 2 * (N_IN + 2))
        silu_done = signal("silu_done", 2 * N_IN)
        h_ready = signal("h_ready", 2 * N_IN)
        yb_free = signal("yb_free", 2 * (KB + 2) + (N_MO + 2))
        ssy_done = signal("ssy_done", 3)
        std_y = signal("std_y", 3)
        x_upd = signal("x_upd", 3 * KB)
        x_sq = signal("x_sq", 3 * KB, KB)
        ssx_done = signal("ssx_done", 3, 1)
        std_x = signal("std_x", 3)
        a_f32 = signal("a_f32", 3 * KB)
        a_round = signal("a_round", 3 * KB)
        a_ready = signal("a_ready", 3 * KB)
        mix_evac = signal("mix_evac", N_MI + 2)
        zeroed = signal("zeroed", 2)
        lrw_round = signal("lrw_round")
        lrw_ready = signal("lrw_ready")
        pool_past = signal("pool_past", 7)
        outs_done = signal("outs_done")
        c_copied = signal("c_copied")
        lr_sum = signal("lr_sum")
        lr_ready = signal("lr_ready")
        gate_sum = signal("gate_sum")
        gate_n = signal("gate_n")
        gate_l = signal("gate_l")
        gate_b = signal("gate_b")
        gate_e = signal("gate_e")
        qz_ready = signal("qz_ready")
        kv_t = signal("kv_t", 6)
        kv_k = signal("kv_k", 3)
        kv_v = signal("kv_v", 3)
        zn_sum = signal("zn_sum")
        zn_ready = signal("zn_ready")
        mean_sum = signal("mean_sum")
        dev_ready = signal("dev_ready")
        var_sum = signal("var_sum")
        gm_std = signal("gm_std")
        vn_f = signal("vn_f")
        q_staged = signal("q_staged", B // 2)
        kt_t = signal("kt_t", B * NPG)
        kt_ready = signal("kt_ready", B * NPG)
        z_free = signal("z_free", B // 2 + 1)
        gm_t = signal("gm_t", 4)
        gm_tc = signal("gm_tc", 4)
        wss_sum = signal("wss_sum")
        wss_ready = signal("wss_ready")
        gs_sum = signal("gs_sum", 3)
        gm_done = signal("gm_done")
        gla_in = signal("gla_in")
        gla_t = signal("gla_t", 3)
        gla_tc = signal("gla_tc", 3)
        att_sum = signal("att_sum", 3)
        att_ready = signal("att_ready", 3)
        s_sum = signal("s_sum", CPB)
        s_ready = signal("s_ready", CPB)
        vm_ready = signal("vm_ready", GP)
        ds_sum = signal("ds_sum", GP)
        s0_new = signal("s0_new", GP)
        o_sum = signal("o_sum", 3)
        o_sq = signal("o_sq")
        oss_sum = signal("oss_sum")
        o_std = signal("o_std")
        g_silu = signal("g_silu")
        gla_done = signal("gla_done")
        zp_sum = signal("zp_sum", PR)
        zp_evac = signal("zp_evac", PR)
        sp_n = signal("sp_n", 3)
        sp_l = signal("sp_l", 3)
        sp_ready = signal("sp_ready", 3)
        c_sum = signal("c_sum", 3)
        c_sub = signal("c_sub", 3)
        A_ready = signal("A_ready", 3)
        staged = signal("staged", B // 2)
        op_sum = signal("op_sum", PR)
        op_evac = signal("op_evac", PR)
        heads_round = signal("heads_round")
        heads_ready = signal("heads_ready")
        out_t = signal("out_t")
        out_copied = signal("out_copied")
        k_out = signal("k_out")
        v_out = signal("v_out")
        gmv_out = signal("gmv_out")
        sp_out = signal("sp_out")
        ss_out = signal("ss_out")
        y_out = signal("y_out")
        
        ROWS = 3 + 7 * L + PT_ + 1

        block = ctx.enter_context(nc.Block())

        def halves(phase):
            return [(0, 768), (1024, 640)] if phase == "out" else [(0, 1024), (1024, 1024)]

        @block.sync
        def _(sp):
            def weights(l, pos, j, slot, parts):
                sp.wait_ge(lo_done.sem, lo_done.at(l, 2 * pos - 2) + 2 * j)
                for h, src in enumerate(parts):
                    n = src.shape[1] * src.shape[2]
                    dst = raw[:, slot, 1024 * h:1024 * h + n].rearrange("p (k c) -> p k c", c=P)
                    sp.dma_start(dst, src).then_inc(raw_in[slot][h].sem, 16)

            def ffn_in(l, n, j, slot):
                cols = [ffn_w_in[l, n, :, ds(j * P + h * FF, P)] if not isinstance(j, int)
                        else ffn_w_in[l, n, :, j * P + h * FF:j * P + h * FF + P] for h in (0, 1)]
                weights(l, POS_IN[n], j, slot, [c.rearrange("(k p) c -> p k c", p=P) for c in cols])

            def ffn_out(l, n, m, part, slot, q):
                rows = [(11 * part, 6), (11 * part + 6, 5)]
                weights(l, POS_OUT[n], q, slot, [
                    ffn_w_out[l, n, r * P:(r + k) * P, ds(m * P, P)].rearrange("(k p) c -> p k c", p=P)
                    for r, k in rows])

            def mix(l, w, pos, j, slot, col):
                weights(l, pos, j, slot, [w[l, :, ds(col + h * P, P)].rearrange("(k p) c -> p k c", p=P)
                                          for h in (0, 1)])

            def room(l, dp, c):
                sp.wait_ge(direct_used.sem, direct_used.at(l, dp - 3) + c)

            def cond_load(lc, i, c, slot):
                for k in range(4):
                    r0 = (slot % 2) * (D // 2) + k * P
                    src = cond_w[lc, r0:r0 + P, ds(i * 3 * D + c * 1024 + (slot // 2) * 512, 512)]
                    sp.dma_start(direct[:, slot, 512 * k:512 * k + 512], src).then_inc(direct_in[slot].sem, 16)

            def cond(lc, l, i, c, slot):
                room(l, DP_C[i], c * 4 + slot)
                cond_load(lc, i, c, slot)

            def page_loop(l, cache, dp):
                with sp.Fori(0, NPC // 4) as i:
                    for q in range(4):
                        room(l, dp, i * 4 + q)
                        for t in range(4):
                            page = sp.value_load(pages[0:1, ds(i * 16 + 4 * q + t, 1)], min_val=0,
                                                 max_val=NPOOL - 1)
                            src = cache[l, ds(page, 1), :, :, :].rearrange("o s h d -> s (o h d)")
                            sp.dma_start(direct[:, q, 512 * t:512 * t + 512], src)\
                                .then_inc(direct_in[q].sem, 16)

            def ffn(l, n, conds_in, conds_out):
                with sp.Fori(0, NCH // 4) as i:
                    for s in range(4):
                        ffn_in(l, n, i * 4 + s, s % 2)
                        cond(*conds_in, i, s)
                with sp.Fori(0, (N_IN - NCH) // 2) as i:
                    for s in range(2):
                        ffn_in(l, n, i * 2 + s + NCH, s)
                if conds_out:
                    with sp.Fori(0, NCH // 4) as i:
                        for s in range(4):
                            ffn_out(l, n, i * 2 + s // 2, s % 2, s % 2, i * 4 + s)
                            cond(*conds_out, i, s)
                    with sp.Fori(NCH // 4, N_OUT // 4) as i:
                        for s in range(4):
                            ffn_out(l, n, i * 2 + s // 2, s % 2, s % 2, i * 4 + s)
                else:
                    with sp.Fori(0, N_OUT // 4) as i:
                        for s in range(4):
                            ffn_out(l, n, i * 2 + s // 2, s % 2, s % 2, i * 4 + s)

            sp.dma_start(pages[:, :], page_table.rearrange("b n -> (b n)").unsqueeze(0)).then_inc(rows_in.sem, 16)
            sp.dma_start(ctok[0:1, :], c_prompt).then_inc(rows_in.sem, 16)
            sp.dma_start(ctok[1:NC, :], c_sample).then_inc(rows_in.sem, 16)
            for layer in range(L):
                for r, n, src in ((V_CB, 72, cond_b[layer].rearrange("(r p) -> r p", p=P)),
                                  (V_PRE, 24, norm_pre[layer].rearrange("i (r p) -> (i r) p", p=P)),
                                  (V_POST, 24, norm_post[layer].rearrange("i (r p) -> (i r) p", p=P)),
                                  (V_GB, 2, gla_b_gate[layer].rearrange("(r p) -> r p", p=P)),
                                  (V_GN, 2, gla_norm[layer].rearrange("(r p) -> r p", p=P)),
                                  (V_LW, 2, gm_ln_w[layer].rearrange("(r p) -> r p", p=P)),
                                  (V_LB, 2, gm_ln_b[layer].rearrange("(r p) -> r p", p=P))):
                    sp.dma_start(vrow[r:r + n, layer, :], src).then_inc(rows_in.sem, 16)
            for i in range(PT_):
                sp.dma_start(xtok[:, i, :], x_prompt[0, i * P:i * P + P, :]).then_inc(rows_in.sem, 16)
            sp.dma_start(xtok[0:NS, 2, :], x_sample.rearrange("b t d -> (b t) d")).then_inc(rows_in.sem, 16)
            with sp.Fori(0, NCH // 4) as i:
                for s in range(4):
                    sp.wait_ge(direct_used.sem, i * 4 + s + 1)
                    cond_load(0, 0, i, s)
            sp.wait_ge(rows_in.sem, ROWS * 16)

            with sp.Fori(0, L) as l:
                ffn(l, 0, (l, l, 1), (l, l, 2))
                with sp.Fori(0, LRC // 512) as i:
                    for s in range(2):
                        mix(l, mix_w_in, POS_MI, i * 2 + s, s, i * 512 + s * 256)
                for i, c in ((2, 2), (3, 4), (4, 3), (5, 5)):
                    for s in range(2):
                        mix(l, mix_w_in, POS_MI, i * 2 + s, s, c * 512 + s * 256 + LR)
                for s in range(2):
                    mix(l, mix_w_out, POS_MO, s, s, s * 256)
                page_loop(l, cache_sb_k, DP_K)
                page_loop(l, cache_sb_v, DP_V)
                for s in range(2):
                    mix(l, mix_w_out, POS_MO, 2 + s, s, (2 + s) * 256)
                ffn(l, 1, (L - 1, l, 0), None)
            sp.wait_ge(out_copied.sem, 1)
            for i in range(PT_):
                sp.dma_start(y_prompt[0, i * P:i * P + P, :], xtok[:, i, :]).then_inc(y_out.sem, 16)
            sp.dma_start(y_sample.rearrange("b t d -> (b t) d"), xtok[0:NS, 2, :]).then_inc(y_out.sem, 16)
            sp.wait_ge(y_out.sem, 48)

        @block.tensor
        def _(pe):
            def products(out, slot, word, src_hi, src_lo, k0, n, begins, ends):
                for i in range(n):
                    at_ = word + i * P
                    whi, wlo = w_hi[:, slot, at_:at_ + P], w_lo[:, slot, at_:at_ + P]
                    hi, lo = src_hi[:, k0 + i, :], src_lo[:, k0 + i, :]
                    pe.matmul(out, whi, hi, start=begins and i == 0, stop=False)
                    pe.matmul(out, whi, lo, start=False, stop=False)
                    last = pe.matmul(out, wlo, hi, start=False, stop=ends and i == n - 1)
                return last

            cond_sums = PS[:, 6:8, :].rearrange("p a b -> p (a b)")

            def cond_chunk(l, x, dp, c, slot):
                k = direct_in[slot]
                pair, half = divmod(slot, 2)
                if l is None:
                    pe.wait_ge(k.sem, c * 64 + 64)
                else:
                    pe.wait_ge(k.sem, k.at(l, dp // 4 + 1) * 64 + c * 64)
                if half == 0:
                    if l is None:
                        pe.wait_ge(cond_copied.sem, c * 2 + pair + 1)
                    else:
                        pe.wait_ge(cond_copied.sem, cond_copied.at(l, 6 * x - 1 + pair) + c * 2)
                for kb in range(4):
                    for g in range(4):
                        last = pe.matmul(PS[32 * g:32 * g + 32, 6 + pair, 0:P],
                                         cT[:, 4 * half + kb, :],
                                         direct[:, slot, kb * 512 + g * P:kb * 512 + g * P + P],
                                         start=half == 0 and kb == 0, stop=half == 1 and kb == 3)
                last.then_inc(direct_used.sem, 1)

            def cond_turn():
                for q in range(NCH // 2):
                    last = pe.transpose(cond_sums[:, q * P:q * P + P], crow[:, q * P:q * P + P], ident[:, :])
                last.then_inc(cond_t.sem, 1)

            def in_step(l, n, j, s):
                pos = POS_IN[n]
                par = s % 2
                for h in range(2):
                    pe.wait_ge(lo_done.sem, lo_done.at(l, 2 * pos + h + 1) + 2 * j)
                    if h == 0:
                        pe.wait_ge(gu_free.sem, gu_free.at(l, n * (N_IN + 2) + 1) + j)
                    last = products(PS[:, 2 * h + par, 0:T], par, 1024 * h, a_hi, a_lo, 0, KB, True, True)
                last.then_inc(w_used.sem, 1)

            def out_chunk(l, n, q, s):
                pos = POS_OUT[n]
                par, part, bank = s % 2, s % 2, (s // 2) % 2
                for h, (k, cnt) in enumerate(((0, 6), (6, 5))):
                    pe.wait_ge(lo_done.sem, lo_done.at(l, 2 * pos + h + 1) + 2 * q)
                    last = products(PS[:, bank, 0:T], par, 1024 * h, h_hi, h_lo, 11 * part + k, cnt,
                                    part == 0 and h == 0, part == 1 and h == 1)
                last.then_inc(w_used.sem, 1)

            def ffn(l, n, cond_in, cond_out):
                with pe.Fori(0, NCH // 4) as i:
                    for s in range(4):
                        if s == 0:
                            pe.wait_ge(a_ready.sem, a_ready.at(l, (2 * n + 1) * KB))
                        in_step(l, n, i * 4 + s, s)
                        if s == 0:
                            pe.wait_ge(mod_ready.sem, mod_ready.at(l, cond_in[0]))
                        cond_chunk(l, *cond_in, i, s)
                with pe.Fori(NCH // 2, NCH // 2 + 3) as i:
                    for s in range(2):
                        in_step(l, n, i * 2 + s, s)
                pe.wait_ge(cond_copied.sem, cond_copied.at(l, 6 * cond_in[0] + 6))
                cond_turn()
                with pe.Fori(NCH // 2 + 3, N_IN // 2) as i:
                    for s in range(2):
                        in_step(l, n, i * 2 + s, s)
                yb = YB_OUT[n]

                def squares(m, s, begins=False, ends=False):
                    pe.wait_ge(yb_free.sem, yb_free.at(l, yb + 3) + m)
                    return pe.matmul(PS[:, 5, 0:T], ones[:, :], ysq[:, s, :], start=begins, stop=ends)

                def group(i, with_cond, first=False, turn=False):
                    for s in range(4):
                        if s % 2 == 0:
                            pe.wait_ge(yb_free.sem, yb_free.at(l, yb + 1 + s // 2) + i * 2)
                        if first and s == 0:
                            pe.wait_ge(h_ready.sem, h_ready.at(l, n * N_IN + 11))
                        if first and s == 1:
                            pe.wait_ge(h_ready.sem, h_ready.at(l, (n + 1) * N_IN))
                        out_chunk(l, n, i * 4 + s, s)
                        if with_cond:
                            if s == 0:
                                pe.wait_ge(mod_ready.sem, mod_ready.at(l, cond_out[0]))
                            cond_chunk(l, *cond_out, i, s)
                        if s == 1 and turn:
                            pe.wait_ge(cond_copied.sem, cond_copied.at(l, 6 * cond_out[0] + 6))
                            cond_turn()
                        if s == 1 and not first:
                            squares(i * 2 - 1, 1)
                        if s == 3:
                            squares(i * 2, 0, begins=first)

                NG = N_OUT // 4
                group(0, bool(cond_out), True)
                if cond_out:
                    with pe.Fori(1, NG - 1) as i:
                        group(i, True)
                else:
                    with pe.Fori(1, NG - 1) as i:
                        group(i, False)
                group(NG - 1, False, turn=bool(cond_out))
                squares(2 * NG - 1, 1, ends=True).then_inc(ssy_done.sem, 1)

            def seam_squares(l, seam):
                for k in range(KB):
                    pe.wait_ge(x_sq.sem, x_sq.at(l, seam * KB + k + 1))
                    last = pe.matmul(PS[:, 4, 0:T], ones[:, :], xsq[:, k, :], start=k == 0, stop=k == KB - 1)
                last.then_inc(ssx_done.sem, 1)

            def token_tile(i):
                return (slice(i * P, i * P + P), P) if i < PT_ else (slice(NP, T), NS)

            pe.wait_ge(const_ready.sem, 1)
            pe.wait_ge(c_silu.sem, 1)
            for k in range(KB):
                pe.transpose(PS[:, 0, k * NC:k * NC + NC], ctok[:, k * P:k * P + P], ident[0:NC, 0:NC])
            pe.wait_ge(rows_in.sem, ROWS * 16)
            for layer in range(L):
                pe.transpose(PS[:, 1, layer * P:layer * P + P], vrow[:, layer, :], ident[:, :])
            for i in range(3):
                sl, n = token_tile(i)
                for k in range(KB):
                    last = pe.transpose(PS[:, 2 + 2 * i + k // 4,
                                           (k % 4) * P:(k % 4) * P + n],
                                        xtok[0:n, i, k * P:k * P + P], ident[0:n, 0:n])
            last.then_inc(tposed.sem, 1)
            pe.wait_ge(c_copied.sem, 1)
            pe.wait_ge(start_copied.sem, 1)
            for k in range(KB):
                pe.wait_ge(x_sq.sem, k + 1)
                last = pe.matmul(PS[:, 4, 0:T], ones[:, :], xsq[:, k, :], start=k == 0, stop=k == KB - 1)
            last.then_inc(ssx_done.sem, 1)
            with pe.Fori(0, NCH // 4) as i:
                for s in range(4):
                    cond_chunk(None, 0, 0, i, s)
            pe.wait_ge(cond_copied.sem, 8)
            cond_turn()

            with pe.Fori(0, L) as l:
                ffn(l, 0, (0, DP_C[1]), (1, DP_C[2]))
                seam_squares(l, 0)

                with pe.Fori(0, N_MI // 2) as i:
                    for s in range(2):
                        if s == 0:
                            pe.wait_ge(a_ready.sem, a_ready.at(l, 2 * KB))
                        for h in range(2):
                            pe.wait_ge(lo_done.sem, lo_done.at(l, 2 * POS_MI + h + 1 + 2 * s) + 4 * i)
                            if h == 0:
                                pe.wait_ge(mix_evac.sem, mix_evac.at(l, s + 1) + 2 * i)
                            last = products(PS[:, 2 * s + h, 0:T], s, 1024 * h, a_hi, a_lo, 0, KB, True, True)
                        last.then_inc(w_used.sem, 1)
                pe.wait_ge(lrw_ready.sem, lrw_ready.at(l, 1))
                for k in range(KB):
                    pe.matmul(PS[:, 7, 0:T], lrw_hi[:, k, :], a_hi[:, k, :], start=k == 0, stop=False)
                    pe.matmul(PS[:, 7, 0:T], lrw_hi[:, k, :], a_lo[:, k, :], start=False, stop=False)
                    last = pe.matmul(PS[:, 7, 0:T], lrw_lo[:, k, :], a_hi[:, k, :], start=False, stop=k == KB - 1)
                last.then_inc(lr_sum.sem, 1)

                pe.wait_ge(mix_evac.sem, mix_evac.at(l, N_MI + 2))
                for j in range(GP):
                    last = pe.matmul(PS[:, 6, 0:T], ones[:, :], Fm[:, MV + j, :], start=j == 0, stop=j == GP - 1)
                last.then_inc(mean_sum.sem, 1)
                pe.wait_ge(lr_ready.sem, lr_ready.at(l, 1))
                for j in range(GP):
                    last = pe.matmul(PS[:, 4 + j, 0:T], w2[:, j * P:j * P + P], lr[:, :], start=True, stop=True)
                last.then_inc(gate_sum.sem, 1)
                for i in range(3):
                    sl, n = token_tile(i)
                    for which, f0 in ((0, SK), (1, SV)):
                        bank = 2 + which
                        if i:
                            done = (kv_k, kv_v)[which]
                            pe.wait_ge(done.sem, done.at(l, i))
                        for p in range(PR):
                            last = pe.transpose(PS[0:n, bank, p * P:p * P + P], Fm[:, f0 + p, sl], ident[:, :])
                        last.then_inc(kv_t.sem, 1)
                pe.wait_ge(dev_ready.sem, dev_ready.at(l, 1))
                for j in range(GP):
                    last = pe.matmul(PS[:, 6, 0:T], ones[:, :], dsq[:, j, :], start=j == 0, stop=j == GP - 1)
                last.then_inc(var_sum.sem, 1)
                pe.wait_ge(qz_ready.sem, qz_ready.at(l, 1))
                for p in range(PR):
                    last = pe.matmul(PS[0:NS, 1, 64 * p:64 * p + 64], Fm[:, SK + p, NP:T],
                                     qz[:, p, :, NP:T], start=True, stop=True)
                last.then_inc(zn_sum.sem, 1)

                with pe.Fori(0, B // 2) as i:
                    def turn(n):
                        q, t = divmod(n, 4)
                        if t == 0:
                            pe.wait_ge(direct_in[q].sem, direct_in[q].at(l, DP_K // 4 + 1) * 64 + 64 * i)
                        for p in range(PR):
                            last = pe.transpose(PS[:, 6 + n % 2, p * P:p * P + P],
                                                direct[:, q, 512 * t + p * P:512 * t + p * P + P], ident[:, :])
                        last.then_inc(kt_t.sem, 1)

                    def score(n):
                        pe.wait_ge(kt_ready.sem, kt_ready.at(l, n + 1) + 16 * i)
                        if n == 0:
                            pe.wait_ge(q_staged.sem, q_staged.at(l, 1) + i)
                            pe.wait_ge(z_free.sem, z_free.at(l, 1) + i)
                        b2, page = divmod(n, NPG)
                        for p in range(PR):
                            last = pe.matmul(PS[:, 0, b2 * 256 + page * 32 + p * 8:b2 * 256 + page * 32 + p * 8 + 8],
                                             kt[:, n % 2, p * P:p * P + P],
                                             qd[:, p, :, TS * b2:TS * b2 + TS], start=True, stop=True)
                        if n % 4 == 3:
                            last.then_inc(direct_used.sem, 1)

                    pe.wait_ge(gm_std.sem, gm_std.at(l, 1))
                    turn(0)
                    for n in range(2 * NPG):
                        if n + 1 < 2 * NPG:
                            turn(n + 1)
                        score(n)

                for h in range(GH):
                    if h == 0:
                        pe.wait_ge(ws_in.sem, ws_in.at(l, 1) * 16)
                        pe.wait_ge(kv_v.sem, kv_v.at(l, 3))
                    last = pe.transpose(PS[:, 3, h * P:h * P + P], wsr[:, h, :], ident[:, :])
                last.then_inc(gm_t.sem, 1)
                pe.wait_ge(vn_f.sem, vn_f.at(l, 1))
                pe.wait_ge(gm_tc.sem, gm_tc.at(l, 1))
                for i in range(3):
                    sl, n = token_tile(i)
                    bank = 1 + i % 2
                    if i == 0:
                        pe.wait_ge(zn_ready.sem, zn_ready.at(l, 1))
                        pe.wait_ge(kv_k.sem, kv_k.at(l, 3))
                    if i == 2:
                        pe.wait_ge(gm_tc.sem, gm_tc.at(l, 2))
                    for j in range(GP):
                        last = pe.transpose(PS[0:n, bank, j * P:j * P + P], dm[:, j, sl], ident[:, :])
                    last.then_inc(gm_t.sem, 1)
                pe.matmul(PS[0:NS, 4, 0:GH * TS], rep[:, :, :].rearrange("s b t -> s (b t)"),
                          wst[0:TS, :, 0:TS], start=True, stop=True).then_inc(wss_sum.sem, 1)
                pe.wait_ge(gm_tc.sem, gm_tc.at(l, 4))
                for i in range(PT_):
                    for j in range(GP):
                        last = pe.matmul(PS[:, 1 + i, 256 * j:256 * j + 256], vn[:, i, j * P:j * P + P],
                                         wst[:, 2 * j:2 * j + 2, :], start=True, stop=True)
                    last.then_inc(gs_sum.sem, 1)
                pe.wait_ge(wss_ready.sem, wss_ready.at(l, 1))
                for j in range(GP):
                    last = pe.matmul(PS[:, 3, 64 * j:64 * j + 64], vn[0:NS, 2, j * P:j * P + P],
                                     wss[:, 2 * j:2 * j + 2, :], start=True, stop=True)
                last.then_inc(gs_sum.sem, 1)

                pe.wait_ge(gla_in.sem, gla_in.at(l, 1))
                for i in range(3):
                    sl, n = token_tile(i)
                    if i == 2:
                        pe.wait_ge(gla_tc.sem, gla_tc.at(l, 1))
                    for j in range(GP):
                        pe.transpose(PS[0:n, 6 + i % 2, j * P:j * P + P], Fm[:, GV + j, sl], ident[:, :])
                    for j in range(GP):
                        last = pe.transpose(PS[0:n, 6 + i % 2, 256 + j * P:256 + j * P + P], gt[3][:, j, sl], ident[:, :])
                    last.then_inc(gla_t.sem, 1)
                for i in range(3):
                    sl, n = token_tile(i)
                    bank = (4, 5, 0)[i]
                    if i == 0:
                        pe.wait_ge(wss_ready.sem, wss_ready.at(l, 1))
                    if i == 2:
                        pe.wait_ge(z_free.sem, z_free.at(l, B // 2 + 1))
                    for j in range(GP):
                        last = pe.matmul(PS[0:n, bank, 2 * n * j:2 * n * j + 2 * n], gt[0][:, j, sl],
                                         gqz[:, j, :, sl], start=True, stop=True)
                    last.then_inc(att_sum.sem, 1)
                pe.wait_ge(gm_done.sem, gm_done.at(l, 1))
                pe.wait_ge(gla_tc.sem, gla_tc.at(l, 3))
                for i in range(PT_):
                    pe.wait_ge(att_ready.sem, att_ready.at(l, i + 1))
                    for j in range(GP):
                        last = pe.matmul(PS[:, 1 + i, 256 * j:256 * j + 256], gv[:, i, j * P:j * P + P],
                                         att[:, i, j, :, :], start=j == 0, stop=False)
                    for cc in range(2):
                        c = 2 * i + cc
                        if c:
                            pe.wait_ge(s_ready.sem, s_ready.at(l, c))
                            for j in range(GP):
                                out = PS[:, 1 + i, 256 * j:256 * j + 256].rearrange("p (h t) -> p h t", h=2)
                                last = pe.matmul(out[:, :, cc * GC:cc * GC + GC], S[:, (c - 1) % 2, j, :],
                                                 gqz[:, j, :, c * GC:c * GC + GC], start=False,
                                                 stop=cc == 1 and j == GP - 1)
                        if cc == 1:
                            last.then_inc(o_sum.sem, 1)
                        for j in range(GP):
                            last = pe.matmul(PS[:, 6 + c % 2, j * P:j * P + P], kend[:, c, j * P:j * P + P],
                                             gv[:, i, j * P:j * P + P], start=True, stop=True)
                        last.then_inc(s_sum.sem, 1)
                pe.wait_ge(att_ready.sem, att_ready.at(l, 3))
                pe.wait_ge(s0_in.sem, s0_in.at(l, 1) * 32)
                for j in range(GP):
                    pe.matmul(PS[:, 3, 64 * j:64 * j + 64], gv[0:NS, 2, j * P:j * P + P],
                              att_s[:, j, :, :], start=j == 0, stop=False)
                for j in range(GP):
                    for h in range(2):
                        for b in range(B):
                            at_ = 64 * j + 32 * h + TS * b
                            last = pe.matmul(PS[64 * h:64 * h + 64, 3, at_:at_ + TS], S0[:, b, j, :],
                                             gqz[:, j, h, NP + TS * b:NP + TS * b + TS],
                                             start=False, stop=j == GP - 1 and b == B - 1)
                last.then_inc(o_sum.sem, 1)
                for j in range(GP):
                    pe.wait_ge(vm_ready.sem, vm_ready.at(l, j + 1))
                    if j:
                        pe.wait_ge(s0_new.sem, s0_new.at(l, 1))
                    for q in range(2):
                        last = pe.matmul(PS[:, 4 + q, :], kend[0:NS, CPB, j * P:j * P + P],
                                         vm[:, 4 * q:4 * q + 4, :], start=True, stop=True)
                    last.then_inc(ds_sum.sem, 1)
                pe.wait_ge(o_sq.sem, o_sq.at(l, 1))
                pe.wait_ge(s_ready.sem, s_ready.at(l, CPB))
                for j in range(GP):
                    last = pe.matmul(PS[:, 6 + j, 0:T], head_ones[:, :], gt[2][:, j, :], start=True, stop=True)
                last.then_inc(oss_sum.sem, 1)

                pe.wait_ge(sp_ready.sem, sp_ready.at(l, 1))
                pe.wait_ge(s0_new.sem, s0_new.at(l, GP))
                for i in range(4):
                    pe.matmul(PS[:, i, :], suffix[:, :], sn[:, 512 * i:512 * i + 512], start=True, stop=False)
                    last = pe.matmul(PS[:, i, :], ones[:, :], sm[:, 512 * i:512 * i + 512], start=False, stop=True)
                pe.matmul(PS[0:NS, 4, 0:256], suffix[0:NS, 0:NS], sn[0:NS, 2048:2304], start=True, stop=True)\
                    .then_inc(c_sum.sem, 1)
                pe.wait_ge(gla_done.sem, gla_done.at(l, 1))
                for p in range(PR):
                    if p:
                        pe.wait_ge(zp_evac.sem, zp_evac.at(l, p))
                    pe.matmul(PS[:, 6, :], Fm[:, SK + p, 0:P], qz[:, p, :, 0:NP], start=True, stop=True)
                    pe.matmul(PS[:, 7, 0:256], Fm[:, SK + p, P:NP], qz[:, p, :, P:NP], start=True, stop=True)\
                        .then_inc(zp_sum.sem, 1)
                for g in range(2):
                    pe.wait_ge(sp_ready.sem, sp_ready.at(l, 2 + g))
                    if g == 0:
                        pe.wait_ge(c_sub.sem, c_sub.at(l, 1))
                        pe.wait_ge(zp_evac.sem, zp_evac.at(l, PR))
                    else:
                        pe.wait_ge(c_sub.sem, c_sub.at(l, 2))
                    for p in range(2):
                        top = sn[:, 512 * p:512 * p + 512]
                        low = sn[:, 1024 + 256 * p:1024 + 256 * p + 256]
                        pe.matmul(PS[:, p, :], suffix[:, :], top, start=True, stop=False)
                        pe.matmul(PS[:, p, :].rearrange("p (h q) -> p h q", h=2)[:, :, P:NP], ones[:, :],
                                  low, start=False, stop=True)
                        last = pe.matmul(PS[:, 2, 256 * p:256 * p + 256], suffix[:, :], low, start=True, stop=True)
                    last.then_inc(c_sum.sem, 1)
                for p in range(PR):
                    if p == 0:
                        pe.wait_ge(A_ready.sem, A_ready.at(l, 2))
                        pe.wait_ge(kv_v.sem, kv_v.at(l, 3))
                    if p == 2:
                        pe.wait_ge(A_ready.sem, A_ready.at(l, 3))
                    if p >= 2:
                        pe.wait_ge(op_evac.sem, op_evac.at(l, p - 1))
                    pe.matmul(PS[:, 6 + p % 2, :], sv[:, 0, p * P:p * P + P], zp0[:, 2 * p:2 * p + 2, :],
                              start=True, stop=False)
                    pe.matmul(PS[:, 6 + p % 2, :].rearrange("p (h q) -> p h q", h=2)[:, :, P:NP],
                              sv[:, 1, p * P:p * P + P], zp1[:, 2 * p:2 * p + 2, :],
                              start=False, stop=True).then_inc(op_sum.sem, 1)
                with pe.Fori(0, B // 2) as i:
                    pe.wait_ge(staged.sem, staged.at(l, 1) + i)
                    for p in range(PR):
                        pe.matmul(PS[:, 4, 16 * p:16 * p + 16], sv[0:NS, 2, p * P:p * P + P],
                                  an_st[:, 2 * p:2 * p + 2, :], start=p == 0, stop=False)
                    for q in range(4):
                        pe.wait_ge(direct_in[q].sem, direct_in[q].at(l, DP_V // 4 + 1) * 64 + 64 * i)
                        for t in range(4):
                            b2, page = divmod(4 * q + t, NPG)
                            for p in range(PR):
                                out = PS[:, 4, 16 * p:16 * p + 16].rearrange("p (h c) -> p h c", h=2)
                                last = pe.matmul(out[:, :, TS * b2:TS * b2 + TS],
                                                 direct[:, q, 512 * t + p * P:512 * t + p * P + P],
                                                 a_st[:, b2, page * 32 + 8 * p:page * 32 + 8 * p + 8],
                                                 start=False, stop=4 * q + t == 2 * NPG - 1 and p == PR - 1)
                        last.then_inc(direct_used.sem, 1)

                pe.wait_ge(heads_ready.sem, heads_ready.at(l, 1))
                for j in range(N_MO):
                    s = j % 2
                    for h in range(2):
                        pe.wait_ge(lo_done.sem, lo_done.at(l, 2 * (POS_MO + j) + h + 1))
                        if h == 0:
                            pe.wait_ge(yb_free.sem, yb_free.at(l, KB + 2 + j + 1))
                        last = products(PS[:, 2 * s + h, 0:T], s, 1024 * h, a_hi, a_lo, 0, KB, True, True)
                    last.then_inc(w_used.sem, 1)
                    if j:
                        pe.wait_ge(yb_free.sem, yb_free.at(l, KB + 2 + 2 + j))
                        for h in range(2):
                            last = pe.matmul(PS[:, 5, 0:T], ones[:, :], ysq[:, 2 * ((j - 1) % 2) + h, :], start=j == 1 and h == 0, stop=False)
                pe.wait_ge(yb_free.sem, yb_free.at(l, KB + 2 + 2 + N_MO))
                for h in range(2):
                    last = pe.matmul(PS[:, 5, 0:T], ones[:, :], ysq[:, 2 * ((N_MO - 1) % 2) + h, :], start=False, stop=h == 1)
                last.then_inc(ssy_done.sem, 1)
                seam_squares(l, 1)
                ffn(l, 1, (2, DP_C[0]), None)
                seam_squares(l, 2)
            pe.wait_ge(x_upd.sem, x_upd.at(L, 0))
            for i in range(3):
                sl, n = token_tile(i)
                for k in range(KB):
                    bank = 2 * i + k // 4
                    last = pe.transpose(PS[0:n, bank, (k % 4) * P:(k % 4) * P + P], X[:, k, sl], ident[:, :])
            last.then_inc(out_t.sem, 1)


        @block.scalar
        def _(act):
            def split(l, pos, i, s, kind="in"):
                for h, (at_, n) in enumerate(halves(kind)):
                    k = raw_in[s][h]
                    act.wait_ge(k.sem, k.at(l, pos // 2 + 1) * 16 + i * 16)
                    if h == 0:
                        act.wait_ge(w_used.sem, w_used.at(l, pos + s - 1) + 2 * i)
                    act.activation(w_hi[:, s, at_:at_ + n], raw[:, s, at_:at_ + n], ACT.Copy)\
                        .then_inc(hi_done.sem, 1)

            def ffn(l, n, after):
                pos, out = POS_IN[n], POS_OUT[n]

                def silu(j, s):
                    act.wait_ge(w_used.sem, w_used.at(l, pos + 1) + j)
                    act.wait_ge(gu_free.sem, gu_free.at(l, n * (N_IN + 2) + 1) + j)
                    act.activation(sg[:, s, :], PS[:, s, 0:T], ACT.Silu).then_inc(silu_done.sem, 1)

                with act.Fori(0, N_IN // 2 - 1) as i:
                    for s in range(2):
                        split(l, pos, i + 1, s)
                        silu(i * 2 + s, s)
                for s in range(2):
                    split(l, out, 0, s, "out")
                    silu(N_IN - 2 + s, s)
                act.drain()
                act.sem_inc(yb_free.sem, 2)

                def evac(m, s):
                    act.wait_ge(w_used.sem, w_used.at(l, out + 2) + 2 * m)
                    act.activation(Y[:, ds(m, 1), :] if not isinstance(m, int) else Y[:, m:m + 1, :],
                                   PS[:, s:s + 1, 0:T], ACT.Copy)
                    act.activation(ysq[:, s, :], PS[:, s, 0:T], ACT.Square).then_inc(yb_free.sem, 1)

                with act.Fori(0, KB // 2 - 1) as i:
                    for g in range(2):
                        for s in range(2):
                            split(l, out, 2 * i + 1 + g, s, "out")
                        evac(2 * i + g, g)
                for s in range(2):
                    split(l, out, KB - 1, s, "out")
                evac(KB - 2, 0)
                if after is not None:
                    for s in range(2):
                        split(l, after, 0, s)
                evac(KB - 1, 1)

            def seam_post(l, k):
                act.wait_ge(ssy_done.sem, ssy_done.at(l, k + 1))
                act.activation(std[:, :], PS[:, 5, 0:T], ACT.Sqrt, scale=1.0 / D, bias=eps[:, :])\
                    .then_inc(std_y.sem, 1)
                for kb in range(KB):
                    act.wait_ge(x_upd.sem, x_upd.at(l, k * KB + kb + 1))
                    act.activation(xsq[:, kb, :], X[:, kb, :], ACT.Square).then_inc(x_sq.sem, 1)

            def pre(l, p):
                act.wait_ge(ssx_done.sem, ssx_done.at(l, p))
                act.activation(std[:, :], PS[:, 4, 0:T], ACT.Sqrt, scale=1.0 / D, bias=eps[:, :])\
                    .then_inc(std_x.sem, 1)
                if p == 0:
                    for s in range(2):
                        split(l, POS_IN[0], 0, s)
                for kb in range(KB):
                    act.wait_ge(a_f32.sem, a_f32.at(l, p * KB + kb + 1))
                    act.activation(a_hi[:, kb, :], Y[:, kb, :], ACT.Copy).then_inc(a_round.sem, 1)

            act.wait_ge(rows_in.sem, ROWS * 16)
            act.activation(ctok[:, :], ctok[:, :], ACT.Silu).then_inc(c_silu.sem, 1)
            act.wait_ge(tposed.sem, 1)
            act.activation(cT[:, :, 0:NC], PS[:, 0, 0:KB * NC].rearrange("p (k c) -> p k c", c=NC), ACT.Copy)
            act.activation(vecs[:, :, :], PS[:, 1, 0:L * P].rearrange("p (k c) -> p k c", c=P), ACT.Copy)\
                .then_inc(c_copied.sem, 1)
            act.wait_ge(start_copied.sem, 1)
            for kb in range(KB):
                act.activation(xsq[:, kb, :], X[:, kb, :], ACT.Square).then_inc(x_sq.sem, 1)

            with act.Fori(0, L) as l:
                pre(l, 0)
                ffn(l, 0, POS_MI)
                seam_post(l, 0)
                pre(l, 1)

                act.wait_ge(small_in.sem, small_in.at(l, 1) * 48)
                act.wait_ge(zeroed.sem, zeroed.at(l, 1))
                act.activation(lrw_hi[:, :, 0:LR], lr_raw[:, :, :], ACT.Copy).then_inc(lrw_round.sem, 1)
                act.sem_inc(mix_evac.sem, 2)

                def mix_read(j, s):
                    act.wait_ge(w_used.sem, w_used.at(l, POS_MI + 1) + j)
                    out = Fm[:, 2 * j:2 * j + 2, :] if isinstance(j, int) else Fm[:, ds(2 * j, 2), :]
                    act.activation(out, PS[:, 2 * s:2 * s + 2, 0:T], ACT.Copy).then_inc(mix_evac.sem, 1)

                with act.Fori(0, N_MI // 2 - 1) as i:
                    for s in range(2):
                        split(l, POS_MI, i + 1, s)
                        mix_read(i * 2 + s, s)
                for s in range(2):
                    split(l, POS_MO, 0, s)
                    mix_read(N_MI - 2 + s, s)
                act.wait_ge(lr_sum.sem, lr_sum.at(l, 1))
                act.activation(lr[:, :], PS[0:LR, 7, 0:T], ACT.Copy).then_inc(lr_ready.sem, 1)
                for i in range(3):
                    n = P if i < PT_ else NS
                    act.wait_ge(kv_t.sem, kv_t.at(l, 2 * i + 1))
                    act.activation(kst[0:n, i, :], PS[0:n, 2, :], ACT.Copy).then_inc(kv_k.sem, 1)
                act.wait_ge(var_sum.sem, var_sum.at(l, 1))
                act.activation(std[:, :], PS[:, 6, 0:T], ACT.Sqrt, scale=1.0 / GW, bias=eps[:, :])\
                    .then_inc(gm_std.sem, 1)
                act.preload_act_table_set(SOFTPLUS_TABLES)
                act.wait_ge(gate_n.sem, gate_n.at(l, 1))
                act.activation(gt[1][:, :, :], gt[1][:, :, :], ACT.Exp)
                act.drain()
                act.activation(gt[1][:, :, :], gt[1][:, :, :], ACT.Ln, bias=1.0).then_inc(gate_l.sem, 1)
                act.wait_ge(gate_b.sem, gate_b.at(l, 1))
                act.activation(gt[3][:, :, :], gt[3][:, :, :], ACT.Exp, scale=1.0 / TAU)
                act.activation(gt[0][:, :, :], gt[2][:, :, :], ACT.Exp, scale=-1.0 / TAU)
                act.activation(gt[1][:, :, :], gt[2][:, :, :], ACT.Exp, scale=1.0 / TAU).then_inc(gate_e.sem, 1)

                act.wait_ge(qz_ready.sem, qz_ready.at(l, 1))
                act.wait_ge(kv_t.sem, kv_t.at(l, 6))
                act.sem_inc(z_free.sem, 1)
                with act.Fori(0, B // 2) as i:
                    act.activation(qd[:, :, :, :], qz[:, :, :, ds(i * 2 * TS + NP, 2 * TS)], ACT.Copy)\
                        .then_inc(q_staged.sem, 1)
                    for n in range(2 * NPG):
                        act.wait_ge(kt_t.sem, kt_t.at(l, n + 1) + 2 * NPG * i)
                        act.activation(kt[:, n % 2, :], PS[:, 6 + n % 2, :], ACT.Copy)\
                            .then_inc(kt_ready.sem, 1)
                    act.wait_ge(direct_used.sem, direct_used.at(l, DP_K + 4) + 4 * i)
                    act.activation(z[:, ds(i * 512, 512)], PS[:, 0, :], ACT.Copy, scale=HD ** -0.5)\
                        .then_inc(z_free.sem, 1)

                act.activation(Fm[:, GG:GG + 2, :], Fm[:, GG:GG + 2, :], ACT.Silu).then_inc(g_silu.sem, 1)
                act.wait_ge(oss_sum.sem, oss_sum.at(l, 1))
                act.activation(gt[2][:, :, :], PS[:, 6:8, 0:T], ACT.Sqrt, scale=1.0 / HD, bias=eps[:, :])\
                    .then_inc(o_std.sem, 1)

                act.preload_act_table_set(SOFTPLUS_TABLES)

                def log1p_exp(k, parts):
                    act.wait_ge(sp_n.sem, sp_n.at(l, k))
                    for a in parts:
                        act.activation(a, a, ACT.Exp)
                    act.drain()
                    for i, a in enumerate(parts):
                        last = act.activation(a, a, ACT.Ln, bias=1.0)
                    last.then_inc(sp_l.sem, 1)

                log1p_exp(1, [sn[:, 0:NZ], sn[0:NS, NZ:]])
                act.wait_ge(gmv_out.sem, gmv_out.at(l, 1) * 16)
                for p in range(PR):
                    act.wait_ge(zp_sum.sem, zp_sum.at(l, p + 1))
                    for h in range(2):
                        b_ = sbb[:, 2 * p + h:2 * p + h + 1]
                        act.activation(zp0[:, 2 * p + h, :], PS[:, 6, NP * h:NP * h + NP], ACT.Identity,
                                       scale=HD ** -0.5, bias=b_)
                        last = act.activation(zp1[:, 2 * p + h, :], PS[:, 7, P * h:P * h + P], ACT.Identity,
                                              scale=HD ** -0.5, bias=b_)
                    last.then_inc(zp_evac.sem, 1)
                act.wait_ge(c_sub.sem, c_sub.at(l, 1))
                act.activation(z[:, 0:NZ], z[:, 0:NZ], ACT.Exp)
                act.activation(z[0:NS, NZ:], z[0:NS, NZ:], ACT.Exp).then_inc(A_ready.sem, 1)
                for g in range(2):
                    log1p_exp(2 + g, [sn[:, 0:1536]])
                    act.wait_ge(c_sub.sem, c_sub.at(l, 2 + g))
                    act.activation(zp0[:, 4 * g:4 * g + 4, :], zp0[:, 4 * g:4 * g + 4, :], ACT.Exp)
                    act.activation(zp1[:, 4 * g:4 * g + 4, :], zp1[:, 4 * g:4 * g + 4, :], ACT.Exp)\
                        .then_inc(A_ready.sem, 1)
                act.drain()
                act.wait_ge(k_out.sem, k_out.at(l, 1) * 48)
                with act.Fori(0, B // 2) as i:
                    act.activation(a_st[:, :, :], z[:, ds(i * 512, 512)].rearrange("p (b c) -> p b c", b=2),
                                   ACT.Copy)
                    zn = z[0:NS, NZ:].rearrange("s (h c) -> s h c", c=NS)
                    act.activation(an_st[:, :, :], zn[:, :, ds(i * 2 * TS, 2 * TS)], ACT.Copy)\
                        .then_inc(staged.sem, 1)
                    act.wait_ge(direct_used.sem, direct_used.at(l, DP_V + 4) + 4 * i)
                    for h in range(2):
                        o = PS[64 * h:64 * h + 64, 4, 0:64].rearrange("d (p h c) -> d p h c", p=PR, h=2)
                        act.activation(Y[64 * h:64 * h + 64, 4:8, ds(i * 2 * TS + NP, 2 * TS)],
                                       o[:, :, h, :], ACT.Copy)
                act.drain()
                act.wait_ge(gla_done.sem, gla_done.at(l, 1))
                act.wait_ge(op_evac.sem, op_evac.at(l, PR))
                act.activation(a_hi[:, :, :], Y[:, :, :], ACT.Copy).then_inc(heads_round.sem, 1)

                act.sem_inc(yb_free.sem, 2)
                for j in range(N_MO):
                    if j < 2:
                        split(l, POS_MO, 1, j % 2)
                    else:
                        split(l, POS_IN[1], 0, j % 2)
                    act.wait_ge(w_used.sem, w_used.at(l, POS_MO + j + 1))
                    act.activation(Y[:, 2 * j:2 * j + 2, :], PS[:, 2 * (j % 2):2 * (j % 2) + 2, 0:T], ACT.Copy)
                    act.activation(ysq[:, 2 * (j % 2):2 * (j % 2) + 2, :], PS[:, 2 * (j % 2):2 * (j % 2) + 2, 0:T],
                                   ACT.Square).then_inc(yb_free.sem, 1)
                seam_post(l, 1)
                pre(l, 2)
                ffn(l, 1, None)
                seam_post(l, 2)
            act.wait_ge(out_t.sem, 1)
            for i in range(3):
                n = P if i < PT_ else NS
                last = act.activation(xtok[0:n, i, :], PS[0:n, 2 * i:2 * i + 2, :].rearrange("p a b -> p (a b)"),
                                      ACT.Copy)
            last.then_inc(out_copied.sem, 1)

        @block.vector
        def _(dve):
            tt, ts_, stt, cp = dve.tensor_tensor, dve.tensor_scalar, dve.scalar_tensor_tensor, dve.tensor_copy

            def split(l, pos, i, s, kind="in"):
                for h, (at_, n) in enumerate(halves(kind)):
                    dve.wait_ge(hi_done.sem, hi_done.at(l, 2 * (pos + s) + h + 1) + 4 * i)
                    tt(w_lo[:, s, at_:at_ + n], raw[:, s, at_:at_ + n], w_hi[:, s, at_:at_ + n],
                       ALU.subtract).then_inc(lo_done.sem, 1)

            def copy_sums(used, i, pair):
                dve.wait_ge(direct_used.sem, used + 2 * pair + 2 + 4 * i)
                cp(crow[:, ds(i * 2 * P + pair * P, P)], PS[:, 6 + pair, 0:P]).then_inc(cond_copied.sem, 1)

            def modulation(i, v):
                m = M[:, i, :, :]
                acc = PS[:, 6:8, :].rearrange("p a (k c) -> p (a k) c", c=32)[:, 0:NF, 0:NC]

                def col(a, n):
                    return v(a, n).unsqueeze(2).to_broadcast([P, n, NC])
                tt(m, acc, col(V_CB + NF * i, NF), ALU.add)
                dve.drain()
                stt(m[:, KB:2 * KB, :], m[:, KB:2 * KB, :], 1.0, col(V_PRE + KB * i, KB), ALU.add, ALU.mult)
                stt(m[:, 2 * KB:, :], m[:, 2 * KB:, :], 1.0 if i == 1 else 0.5, col(V_POST + KB * i, KB),
                    ALU.mult, ALU.mult).then_inc(mod_ready.sem, 1)

            def sample(t, k0=0, k1=KB):
                return t[:, k0:k1, NP:T].rearrange("p k (b t) -> p k b t", t=TS)

            def per_sample(i, k0):
                return M[:, i, k0:k0 + KB, 1:NC].unsqueeze(3).to_broadcast([P, KB, B, TS])

            def over_blocks(row, n=KB):
                return row.unsqueeze(1).to_broadcast([P, n, T])

            def seam_post(l, k):
                dve.wait_ge(std_y.sem, std_y.at(l, k + 1))
                dve.reciprocal(rstd[:, :], std[:, :])
                dve.drain()
                tt(Y[:, :, :], Y[:, :, :], over_blocks(rstd[:, :]), ALU.mult)
                dve.drain()
                tt(sample(Y), sample(Y), per_sample(k, 2 * KB), ALU.mult)
                dve.drain()
                tt(sample(X), sample(X), sample(Y), ALU.add)
                for kb in range(KB):
                    stt(X[:, kb, 0:NP], Y[:, kb, 0:NP], M[:, k, 2 * KB + kb, 0:1], X[:, kb, 0:NP],
                        ALU.mult, ALU.add).then_inc(x_upd.sem, 1)

            def pre(l, p):
                dve.wait_ge(std_x.sem, std_x.at(l, p + 1))
                dve.reciprocal(rstd[:, :], std[:, :])
                dve.drain()
                tt(Y[:, :, :], X[:, :, :], over_blocks(rstd[:, :]), ALU.mult)
                dve.drain()
                tt(sample(Y), sample(Y), per_sample(p, KB), ALU.mult)
                dve.drain()
                tt(sample(Y), sample(Y), per_sample(p, 0), ALU.add)
                for kb in range(KB):
                    ts_(Y[:, kb, 0:NP], Y[:, kb, 0:NP], M[:, p, KB + kb, 0:1], M[:, p, kb, 0:1],
                        ALU.mult, ALU.add).then_inc(a_f32.sem, 1)
                dve.drain()
                if p == 0:
                    for s in range(2):
                        split(l, POS_IN[0], 0, s)
                for kb in range(KB):
                    dve.wait_ge(a_round.sem, a_round.at(l, p * KB + kb + 1))
                    tt(a_lo[:, kb, :], Y[:, kb, :], a_hi[:, kb, :], ALU.subtract).then_inc(a_ready.sem, 1)

            def ffn(l, n, after):
                pos, out = POS_IN[n], POS_OUT[n]
                dve.sem_inc(gu_free.sem, 2)

                def hidden(j, s):
                    dve.wait_ge(silu_done.sem, silu_done.at(l, n * N_IN + 1) + j)
                    at_ = slice(j, j + 1) if isinstance(j, int) else ds(j, 1)
                    tt(hf[:, s:s + 1, :], sg[:, s:s + 1, :], PS[:, 2 + s:3 + s, 0:T], ALU.mult)\
                        .then_inc(gu_free.sem, 1)
                    dve.drain()
                    cp(h_hi[:, at_, :], hf[:, s:s + 1, :])
                    dve.drain()
                    tt(h_lo[:, at_, :], hf[:, s:s + 1, :], h_hi[:, at_, :], ALU.subtract)\
                        .then_inc(h_ready.sem, 1)

                i_in = 1 if n == 0 else 0
                with dve.Fori(0, NCH // 4) as i:
                    for s in range(4):
                        split(l, pos, i * 2 + (s // 2 + 1), s % 2)
                        hidden(i * 4 + s, s % 2)
                        if s >= 2:
                            copy_sums(direct_used.at(l, DP_C[i_in]), i, s - 2)
                with dve.Fori(NCH // 2, N_IN // 2 - 1) as i:
                    for s in range(2):
                        split(l, pos, i + 1, s)
                        hidden(i * 2 + s, s)
                for s in range(2):
                    split(l, out, 0, s, "out")
                    hidden(N_IN - 2 + s, s)
                dve.wait_ge(cond_t.sem, cond_t.at(l, 1 if n == 0 else 3))
                modulation(i_in, (lambda a, k: vec[:, a:a + k]) if n == 0 else (lambda a, k: vecs[:, L - 1, a:a + k]))
                with dve.Fori(0, KB // 2 - 1) as i:
                    for g in range(2):
                        for s in range(2):
                            split(l, out, 2 * i + 1 + g, s, "out")
                        if n == 0:
                            copy_sums(direct_used.at(l, DP_C[2]), i, g)
                for s in range(2):
                    split(l, out, KB - 1, s, "out")
                if after is not None:
                    for s in range(2):
                        split(l, after, 0, s)
                if n == 0:
                    dve.wait_ge(cond_t.sem, cond_t.at(l, 2))
                    modulation(2, lambda a, k: vec[:, a:a + k])

            dve.sem_inc(lo_done.sem, 4)
            dve.sem_inc(w_used.sem, 2)
            dve.sem_inc(direct_used.sem, 4)
            dve.sem_inc(cond_copied.sem, 2)
            dve.wait_ge(tposed.sem, 1)
            for i in range(3):
                n = P if i < PT_ else NS
                for g in range(2):
                    src = PS[:, 2 + 2 * i + g, :].rearrange("p (k t) -> p k t", k=4)
                    last = cp(X[:, 4 * g:4 * g + 4, P * i:P * i + n], src[:, :, 0:n])
            last.then_inc(start_copied.sem, 1)
            dve.wait_ge(c_copied.sem, 1)
            with dve.Fori(0, NCH // 4) as i:
                for pair in range(2):
                    copy_sums(4, i, pair)
            dve.wait_ge(cond_t.sem, 1)
            modulation(0, lambda a, k: vecs[:, 0, a:a + k])

            with dve.Fori(0, L) as l:
                dve.drain()
                cp(vec[:, :].unsqueeze(1), vecs[:, ds(l, 1), :])
                pre(l, 0)
                ffn(l, 0, POS_MI)
                seam_post(l, 0)
                pre(l, 1)

                dve.wait_ge(lrw_round.sem, lrw_round.at(l, 1))
                tt(lrw_lo[:, :, 0:LR], lr_raw[:, :, :], lrw_hi[:, :, 0:LR], ALU.subtract)\
                    .then_inc(lrw_ready.sem, 1)
                with dve.Fori(0, N_MI // 2 - 1) as i:
                    for s in range(2):
                        split(l, POS_MI, i + 1, s)
                for s in range(2):
                    split(l, POS_MO, 0, s)

                dve.wait_ge(mix_evac.sem, mix_evac.at(l, N_MI + 2))
                dve.wait_ge(zeroed.sem, zeroed.at(l, 1))
                for h in range(2):
                    r = slice(64 * h, 64 * h + 64)
                    last = cp(qz[r, :, h, :], Fm[r, SQ:SQ + PR, :])
                last.then_inc(qz_ready.sem, 1)
                dve.wait_ge(mean_sum.sem, mean_sum.at(l, 1))
                for j in range(GP):
                    stt(dm[:, j, :], PS[:, 6, 0:T], -1.0 / GW, Fm[:, MV + j, :], ALU.mult, ALU.add)
                dve.drain()
                tt(dsq[:, :, :], dm[:, :, :], dm[:, :, :], ALU.mult).then_inc(dev_ready.sem, 1)

                def values(i):
                    n = P if i < PT_ else NS
                    dve.wait_ge(kv_t.sem, kv_t.at(l, 2 * i + 2))
                    cp(sv[0:n, i, :], PS[0:n, 3, :]).then_inc(kv_v.sem, 1)
                values(0)
                dve.wait_ge(gate_sum.sem, gate_sum.at(l, 1))
                for j in range(GP):
                    ts_(gt[0][:, j, :], PS[:, 4 + j, 0:T], vec[:, V_GB + j:V_GB + j + 1], None, ALU.add)
                dve.drain()
                ts_(gt[2][:, :, :], gt[0][:, :, :], 0.0, None, ALU.min)
                dve.drain()
                stt(gt[1][:, :, :], gt[2][:, :, :], 2.0, gt[0][:, :, :], ALU.mult, ALU.subtract)\
                    .then_inc(gate_n.sem, 1)
                values(1)
                values(2)
                zn = z[0:NS, NZ:].rearrange("s (h c) -> s h c", c=NS)
                dve.wait_ge(zn_sum.sem, zn_sum.at(l, 1))
                stt(zn, PS[0:NS, 1, 0:SBH * NS].rearrange("s (h c) -> s h c", c=NS), HD ** -0.5,
                    sbb[0:NS, :].unsqueeze(2).to_broadcast([NS, SBH, NS]), ALU.mult, ALU.add)
                dve.drain()
                tt(zn, zn, neg_mask_s[:, :].unsqueeze(1).to_broadcast([NS, SBH, NS]), ALU.add)\
                    .then_inc(zn_ready.sem, 1)
                dve.wait_ge(gm_std.sem, gm_std.at(l, 1))
                dve.reciprocal(rstd[:, :], std[:, :])
                dve.drain()
                tt(dm[:, :, :], dm[:, :, :], over_blocks(rstd[:, :], GP), ALU.mult)
                dve.drain()
                for j in range(GP):
                    last = ts_(dm[:, j, :], dm[:, j, :], vec[:, V_LW + j:V_LW + j + 1],
                               vec[:, V_LB + j:V_LB + j + 1], ALU.mult, ALU.add)
                last.then_inc(vn_f.sem, 1)
                dve.wait_ge(gate_l.sem, gate_l.at(l, 1))
                tt(gt[0][:, :, :], gt[2][:, :, :], gt[1][:, :, :], ALU.subtract)
                dve.drain()
                for j in range(GP):
                    dve.tensor_tensor_scan(gt[2][:, j, :], restart[:, :], gt[0][:, j, :], 0.0,
                                           ALU.mult, ALU.add)
                dve.drain()
                for t0, t1, c in ((0, NP, GC), (NP, T, TS)):
                    b_ = gt[2][:, :, t0:t1].rearrange("p j (n c) -> p j n c", c=c)
                    d_ = gt[3][:, :, t0:t1].rearrange("p j (n c) -> p j n c", c=c)
                    last = tt(d_, b_[:, :, :, c - 1:c].to_broadcast([P, GP, (t1 - t0) // c, c]), b_,
                              ALU.subtract)
                last.then_inc(gate_b.sem, 1)
                dve.wait_ge(gate_e.sem, gate_e.at(l, 1))
                dve.wait_ge(zeroed.sem, zeroed.at(l, 2))
                tt(gt[3][:, :, :], gt[3][:, :, :], Fm[:, GK:GK + GP, :], ALU.mult)
                tt(gt[0][:, :, :], gt[0][:, :, :], Fm[:, GK:GK + GP, :], ALU.mult)
                for h in range(2):
                    r = slice(64 * h, 64 * h + 64)
                    last = stt(gqz[r, :, h, :], Fm[r, GQ:GQ + GP, :], HD ** -0.5, gt[1][r, :, :],
                               ALU.mult, ALU.mult)
                last.then_inc(gla_in.sem, 1)

                dve.wait_ge(gm_t.sem, gm_t.at(l, 1))
                tt(wst[:, :, :], PS[:, 3, :].rearrange("p (h t) -> p h t", h=GH),
                   causal[:, :].unsqueeze(1).to_broadcast([P, GH, P]), ALU.mult).then_inc(gm_tc.sem, 1)
                for i in range(3):
                    n = P if i < PT_ else NS
                    dve.wait_ge(gm_t.sem, gm_t.at(l, 2 + i))
                    cp(vn[0:n, i, :], PS[0:n, 1 + i % 2, 0:GW]).then_inc(gm_tc.sem, 1)
                dve.wait_ge(wss_sum.sem, wss_sum.at(l, 1))
                tt(wss[:, :, :].rearrange("s h (b t) -> s h b t", t=TS),
                   PS[0:NS, 4, 0:GH * TS].rearrange("s (h t) -> s h t", h=GH).unsqueeze(2)
                   .to_broadcast([NS, GH, B, TS]),
                   same_s[:, :].unsqueeze(1).unsqueeze(3).to_broadcast([NS, GH, B, TS]), ALU.mult)\
                    .then_inc(wss_ready.sem, 1)
                dve.wait_ge(k_out.sem, k_out.at(l, 1) * 48)
                dve.wait_ge(bs_in.sem, bs_in.at(l, 1) * 64)
                for i in range(3):
                    dve.wait_ge(gs_sum.sem, gs_sum.at(l, 1 + i))
                    for h in range(2):
                        r = slice(64 * h, 64 * h + 64)
                        if i < PT_:
                            g = PS[r, 1 + i, :].rearrange("p (j h t) -> p j h t", j=GP, h=2)[:, :, h, :]
                            tt(Y[r, 2:4, P * i:P * i + P], g, bs[r, :, :], ALU.add)
                        else:
                            g = PS[r, 3, 0:128].rearrange("p (j h b t) -> p j h b t", j=GP, h=2, t=TS)[:, :, h, :, :]
                            tt(sample(Y, 2, 4)[r], g,
                               bs[r, :, 0:TS].unsqueeze(2).to_broadcast([64, GP, B, TS]), ALU.add)
                dve.drain()
                tt(Y[:, 2:4, :], Y[:, 2:4, :], Fm[:, MU:MU + 2, :], ALU.mult).then_inc(gm_done.sem, 1)

                for i in range(3):
                    dve.wait_ge(gla_t.sem, gla_t.at(l, 1 + i))
                    src = PS[:, 6 + i % 2, :]
                    if i < PT_:
                        cp(gv[:, i, :], src[:, 0:GW])
                        cp(kend[0:64, 2 * i, :], src[0:64, GW:2 * GW])
                        last = cp(kend[64:P, 2 * i + 1, :], src[64:P, GW:2 * GW])
                    else:
                        cp(gv[0:NS, i, :], src[0:NS, 0:GW])
                        last = cp(kend[0:NS, CPB, :], src[0:NS, GW:2 * GW])
                    last.then_inc(gla_tc.sem, 1)
                for i in range(3):
                    dve.wait_ge(att_sum.sem, att_sum.at(l, 1 + i))
                    if i < PT_:
                        tt(att[:, i, :, :, :].rearrange("p j h t -> p (j h) t"),
                           PS[:, 4 + i, :].rearrange("p (g t) -> p g t", t=P),
                           gla_mask[:, :].unsqueeze(1).to_broadcast([P, GH, P]), ALU.mult)\
                            .then_inc(att_ready.sem, 1)
                    else:
                        tt(att_s[:, :, :, :].rearrange("p j h t -> p (j h) t"),
                           PS[0:NS, 0, 0:GH * NS].rearrange("p (g t) -> p g t", t=NS),
                           gla_mask_s[:, :].unsqueeze(1).to_broadcast([NS, GH, NS]), ALU.mult)\
                            .then_inc(att_ready.sem, 1)
                for c in range(CPB):
                    dve.drain()
                    dve.wait_ge(s_sum.sem, s_sum.at(l, c + 1))
                    if c == 0:
                        cp(S[:, 0, :, :], PS[:, 6, 0:GP * P].rearrange("p (j v) -> p j v", j=GP))\
                            .then_inc(s_ready.sem, 1)
                    else:
                        for j in range(GP):
                            e_ = GC * c + GC - 1
                            last = stt(S[:, c % 2, j, :], S[:, (c - 1) % 2, j, :], gt[1][:, j, e_:e_ + 1],
                                       PS[:, 6 + c % 2, j * P:j * P + P], ALU.mult, ALU.add)
                        last.then_inc(s_ready.sem, 1)

                def spread(j):
                    tt(vm[:, :, :], gv[0:NS, 2, j * P:j * P + P].unsqueeze(1).to_broadcast([NS, B, P]),
                       same_s[:, :].unsqueeze(2).to_broadcast([NS, B, P]), ALU.mult).then_inc(vm_ready.sem, 1)
                spread(0)
                for i in range(3):
                    dve.wait_ge(o_sum.sem, o_sum.at(l, 1 + i))
                    for h in range(2):
                        r = slice(64 * h, 64 * h + 64)
                        n = P if i < PT_ else NS
                        src = PS[r, 1 + i, 0:4 * n].rearrange("p (j h t) -> p j h t", j=GP, h=2)[:, :, h, :]
                        cp(gt[0][r, :, P * i:P * i + n], src)
                dve.drain()
                tt(gt[2][:, :, :], gt[0][:, :, :], gt[0][:, :, :], ALU.mult).then_inc(o_sq.sem, 1)
                for j in range(GP):
                    dve.wait_ge(ds_sum.sem, ds_sum.at(l, j + 1))
                    if j == 0:
                        dve.wait_ge(s0_in.sem, s0_in.at(l, 1) * 32)
                    e_ = gt[1][:, j, NP + TS - 1:T:TS]
                    tt(S0[:, :, j, :], S0[:, :, j, :], e_.unsqueeze(2).to_broadcast([P, B, HD]), ALU.mult)
                    dve.drain()
                    for h in range(2):
                        r = slice(64 * h, 64 * h + 64)
                        for q in range(2):
                            src = PS[r, 4 + q, :].rearrange("p (b v) -> p b v", b=4)[:, :, 64 * h:64 * h + 64]
                            last = tt(S0[r, 4 * q:4 * q + 4, j, :], S0[r, 4 * q:4 * q + 4, j, :], src, ALU.add)
                    last.then_inc(s0_new.sem, 1)
                    if j == 0:
                        spread(1)
                dve.wait_ge(o_std.sem, o_std.at(l, 1))
                dve.wait_ge(g_silu.sem, g_silu.at(l, 1))
                dve.reciprocal(gt[2][:, :, :], gt[2][:, :, :])
                dve.drain()
                tt(gt[0][:, :, :], gt[0][:, :, :], gt[2][:, :, :], ALU.mult)
                dve.drain()
                for j in range(GP):
                    last = stt(Y[:, j, :], gt[0][:, j, :], vec[:, V_GN + j:V_GN + j + 1], Fm[:, GG + j, :],
                               ALU.mult, ALU.mult)
                last.then_inc(gla_done.sem, 1)
                dve.drain()

                dve.wait_ge(z_free.sem, z_free.at(l, B // 2 + 1))
                zh = z[:, 0:NZ].rearrange("p (n h t) -> p n h t", h=SBH, t=TS)
                tt(zh, zh, sbb[:, :].unsqueeze(1).unsqueeze(3).to_broadcast([P, B * NPG, SBH, TS]), ALU.add)
                dve.drain()
                parts = [(z[:, 0:NZ], sm[:, 0:NZ], sn[:, 0:NZ]), (z[0:NS, NZ:], sm[0:NS, NZ:], sn[0:NS, NZ:])]

                def softplus(k, parts):
                    for a, m, n in parts:
                        ts_(m, a, 0.0, None, ALU.max)
                    dve.drain()
                    for a, m, n in parts:
                        last = stt(n, m, -2.0, a, ALU.mult, ALU.add)
                    last.then_inc(sp_n.sem, 1)
                    dve.wait_ge(sp_l.sem, sp_l.at(l, k))
                    for i, (a, m, n) in enumerate(parts):
                        last = tt(n, m, n, ALU.add)
                    return last

                softplus(1, parts)
                dve.drain()
                pm = sm[:, 0:NZ].rearrange("p (b g c) -> p b g c", b=B, g=NPG)
                pn = sn[:, 0:NZ].rearrange("p (b g c) -> p b g c", b=B, g=NPG)
                dve.memset(pm[:, :, NPG - 1, :], 0.0)
                dve.drain()
                cp(pm[0:NS, :, NPG - 1, :].rearrange("s b (h t) -> s b h t", t=TS),
                   sn[0:NS, NZ:].rearrange("s (h b t) -> s b h t", h=SBH, t=TS))
                for g in range(NPG - 2, -1, -1):
                    dve.drain()
                    last = tt(pm[:, :, g, :], pm[:, :, g + 1, :], pn[:, :, g + 1, :], ALU.add)
                last.then_inc(sp_ready.sem, 1)
                dve.wait_ge(c_sum.sem, c_sum.at(l, 1))
                tt(z[:, 0:NZ].rearrange("p (a b) -> p a b", a=4), z[:, 0:NZ].rearrange("p (a b) -> p a b", a=4),
                   PS[:, 0:4, :], ALU.subtract)
                tt(z[0:NS, NZ:], z[0:NS, NZ:], PS[0:NS, 4, 0:256], ALU.subtract).then_inc(c_sub.sem, 1)
                dve.wait_ge(zp_evac.sem, zp_evac.at(l, PR))
                neg8 = neg_mask[:, :].unsqueeze(1).to_broadcast([P, SBH, P])
                tt(zp0[:, :, 0:P], zp0[:, :, 0:P], neg8, ALU.add)
                tt(zp1[:, :, :], zp1[:, :, :], neg8, ALU.add)
                dve.drain()
                for g in range(2):
                    z0, z1 = zp0[:, 4 * g:4 * g + 4, :], zp1[:, 4 * g:4 * g + 4, :]
                    f0 = lambda t: t[:, 0:1024].rearrange("p (h q) -> p h q", h=4)
                    f1 = lambda t: t[:, 1024:1536].rearrange("p (h q) -> p h q", h=4)
                    softplus(2 + g, [(z0, f0(sm), f0(sn)), (z1, f1(sm), f1(sn))]).then_inc(sp_ready.sem, 1)
                    dve.wait_ge(c_sum.sem, c_sum.at(l, 2 + g))
                    tt(z0.rearrange("p (a h) q -> p a (h q)", a=2), z0.rearrange("p (a h) q -> p a (h q)", a=2),
                       PS[:, 0:2, :], ALU.subtract)
                    tt(z1.rearrange("p h q -> p (h q)"), z1.rearrange("p h q -> p (h q)"),
                       PS[:, 2, :], ALU.subtract).then_inc(c_sub.sem, 1)
                for p in range(PR):
                    dve.wait_ge(op_sum.sem, op_sum.at(l, p + 1))
                    for h in range(2):
                        r = slice(64 * h, 64 * h + 64)
                        last = cp(Y[r, 4 + p, 0:NP], PS[r, 6 + p % 2, NP * h:NP * h + NP])
                    last.then_inc(op_evac.sem, 1)
                dve.drain()
                dve.wait_ge(heads_round.sem, heads_round.at(l, 1))
                tt(a_lo[:, :, :], Y[:, :, :], a_hi[:, :, :], ALU.subtract).then_inc(heads_ready.sem, 1)

                for s in range(2):
                    split(l, POS_MO, 1, s)
                for s in range(2):
                    split(l, POS_IN[1], 0, s)
                seam_post(l, 1)
                pre(l, 2)
                dve.wait_ge(outs_done.sem, outs_done.at(l, 1))
                ffn(l, 1, None)
                seam_post(l, 2)

        @block.gpsimd
        def _(pool):
            def select(t, src, pattern, op, base, cm, fill):
                pool.drain()
                return pool.affine_select(out=t, in_=src, compare_op=op, fill=fill, base=base,
                                          pattern=pattern, channel_multiplier=cm)

            ge, gt_, ne = ALU.is_ge, ALU.is_gt, ALU.not_equal
            pool.memset(eps[:, :], EPS)
            pool.memset(cT[:, :, :], 0.0)
            pool.memset(ones[:, :], 1.0)
            pool.memset(ident[:, :], 0.0)
            pool.memset(rep[:, :, :], 0.0)
            pool.memset(head_ones[:, :], 0.0)
            pool.memset(neg_mask[:, :], 0.0)
            pool.memset(neg_mask_s[:, :], 0.0)
            pool.memset(same_s[:, :], 1.0)
            pool.memset(gla_mask_s[:, :], 1.0)
            pool.memset(restart[:, :], 1.0)
            select(ident[:, :], ident[:, :], [[-1, P]], ne, 0, 1, 1.0)
            select(rep[:, :, :], rep[:, :, :], [[0, B], [-1, TS]], ne, 0, 1, 1.0)
            pool.memset(head_ones[0:64, 0:64], 1.0)
            pool.memset(head_ones[64:P, 64:P], 1.0)
            pool.drain()
            pool.memset(restart[:, 0:NP:GC], 0.0)
            pool.drain()
            pool.memset(restart[:, NP:T:TS], 0.0)
            select(suffix[:, :], ones[:, :], [[-1, P]], ge, 0, 1, 0.0)
            select(causal[:, :], ones[:, :], [[1, P]], ge, 0, -1, 0.0)
            select(gla_mask[:, :], ones[:, :], [[1, P]], ge, 0, -1, 0.0)
            pool.drain()
            pool.memset(gla_mask[0:64, 64:P], 0.0)
            select(neg_mask[:, :], neg_mask[:, :], [[1, P]], gt_, 0, -1, MASKED)
            select(same_s[:, :], same_s[:, :], [[-TS, B]], ge, 0, 1, 0.0)
            select(same_s[:, :], same_s[:, :], [[TS, B]], ge, TS - 1, -1, 0.0)
            for t, op, fill in ((gla_mask_s, ge, 0.0), (neg_mask_s, gt_, MASKED)):
                select(t[:, :], t[:, :], [[1, NS]], op, 0, -1, fill)
                v = t[:, :].rearrange("s (b t) -> s b t", t=TS)
                select(v, v, [[-TS, B], [0, TS]], ge, 0, 1, fill)
                last = select(v, v, [[TS, B], [0, TS]], ge, TS - 1, -1, fill)
            last.then_inc(const_ready.sem, 1)

            def after(sig, l, k):
                pool.wait_ge(sig.sem, sig.at(l, k))
                pool.sem_inc(pool_past.sem, 1)

            with pool.Fori(0, L) as l:
                after(ssy_done, l, 1)
                lrc = mix_w_in[l, :, LRC:LRC + LR].rearrange("(k p) c -> p k c", p=P)
                pool.dma_start(lr_raw[:, :, :], lrc).then_inc(small_in.sem, 16)
                pool.dma_start(w2[:, :], gla_w_gate2[l, :, :]).then_inc(small_in.sem, 16)
                pool.dma_start(sbb[:, :], sb_bias[l, :].partition_broadcast(P)).then_inc(small_in.sem, 16)
                pool.memset(lrw_hi[:, :, :].bitcast(F32), 0.0)
                pool.memset(lrw_lo[:, :, :].bitcast(F32), 0.0)
                pool.memset(qz[:, :, :, :], 0.0).then_inc(zeroed.sem, 1)
                after(lr_sum, l, 1)
                pool.dma_start(wsr[:, :, :], gm_ws[l, :, :, :].rearrange("h t s -> t h s")).then_inc(ws_in.sem, 16)
                for j in range(GP):
                    for h in range(2):
                        pool.dma_start(bs[64 * h:64 * h + 64, j, :], gm_bs[l, 2 * j + h, :].partition_broadcast(64))\
                            .then_inc(bs_in.sem, 16)
                for j in range(GP):
                    pool.dma_start(S0[:, :, j, :], state_gla[l, :, 2 * j:2 * j + 2, :, :]
                                   .rearrange("b h k v -> (h k) b v")).then_inc(s0_in.sem, 16)
                pool.memset(gqz[:, :, :, :], 0.0)
                pool.memset(kend[:, :, :], 0.0).then_inc(zeroed.sem, 1)
                after(kv_k, l, 3)
                after(kv_v, l, 3)
                for t, pr, sa, done in ((kst, k_prompt, k_sample, k_out), (sv, v_prompt, v_sample, v_out)):
                    for i in range(PT_):
                        pool.dma_start(pr[l, 0, P * i:P * i + P, :, :].rearrange("s h d -> s (h d)"), t[:, i, :])\
                            .then_inc(done.sem, 16)
                    pool.dma_start(sa[l, :, :, :, :].rearrange("b t h d -> (b t) (h d)"), t[0:NS, 2, :])\
                        .then_inc(done.sem, 16)
                after(gm_tc, l, 4)
                pool.dma_start(gm_v_sample[l, :, :, :].rearrange("b t d -> (b t) d"), vn[0:NS, 2, :])\
                    .then_inc(gmv_out.sem, 16)
                after(s_ready, l, CPB)
                for h in range(2):
                    pool.dma_start(s_prompt[l, 0, h::2, :, :].rearrange("j k v -> k j v"),
                                   S[64 * h:64 * h + 64, (CPB - 1) % 2, :, 64 * h:64 * h + 64])\
                        .then_inc(sp_out.sem, 16)
                after(s0_new, l, GP)
                for j in range(GP):
                    pool.dma_start(s_sample[l, :, 2 * j:2 * j + 2, :, :].rearrange("b h k v -> (h k) b v"),
                                   S0[:, :, j, :]).then_inc(ss_out.sem, 16)
                pool.wait_ge(k_out.sem, k_out.at(l, 1) * 48)
                pool.wait_ge(v_out.sem, v_out.at(l, 1) * 48)
                pool.wait_ge(gmv_out.sem, gmv_out.at(l, 1) * 16)
                pool.wait_ge(sp_out.sem, sp_out.at(l, 1) * 32)
                pool.wait_ge(ss_out.sem, ss_out.at(l, 1) * 32)
                pool.sem_inc(outs_done.sem, 1)


INPUTS = ["x_prompt", "x_sample", "c_prompt", "c_sample", "cache_sb_k", "cache_sb_v", "state_gla",
          "page_table", "cond_w", "cond_b", "norm_pre", "norm_post", "ffn_w_in", "ffn_w_out",
          "mix_w_in", "mix_w_out", "gla_w_gate2", "gla_b_gate", "gla_norm", "gm_ln_w", "gm_ln_b",
          "gm_ws", "gm_bs", "sb_bias"]


def kernel(**inputs):
    import concourse.bacc as bacc
    from concourse.bass_utils import run_bass_kernel_spmd

    a = {name: np.ascontiguousarray(inputs[name]) for name in INPUTS}
    depth, _, _, sb_heads, hd = a["cache_sb_k"].shape
    batch, seq, d = a["x_prompt"].shape
    dec, dseq, _ = a["x_sample"].shape
    gh = a["state_gla"].shape[2]
    gm_w = a["gm_ln_w"].shape[1]
    outputs = [(batch, seq, d), (dec, dseq, d), (depth, batch, gh, hd, hd), (depth, dec, gh, hd, hd),
               (depth, batch, seq, sb_heads, hd), (depth, batch, seq, sb_heads, hd),
               (depth, dec, dseq, sb_heads, hd), (depth, dec, dseq, sb_heads, hd),
               (depth, dec, dseq, gm_w)]
    nc = bacc.Bacc("TRN2", target_bir_lowering=False, num_devices=1)
    args = [nc.dram_tensor(f"in_{n}", a[n].shape, mybir.dt.from_np(a[n].dtype), kind="ExternalInput").ap()
            for n in INPUTS]
    args += [nc.dram_tensor(f"out_{i}", s, F32, kind="ExternalOutput").ap() for i, s in enumerate(outputs)]
    decoder_step(nc, *args)
    r = run_bass_kernel_spmd(nc, [{f"in_{n}": a[n] for n in INPUTS}], core_ids=[0])
    return tuple(r.results[0][f"out_{i}"] for i in range(len(outputs)))
```

```python
from contextlib import ExitStack

import numpy as np
import concourse.bass as bass
from concourse import mybir

F32 = mybir.dt.float32
F32R = mybir.dt.float32r
I32 = mybir.dt.int32
ALU = mybir.AluOpType
ACT = mybir.ActivationFunctionType
ds = bass.ds

P = 128
EPS = 1e-6
MASKED = -1e30
TOP_Z = 30.0
LOG_TABLES = "natural_log_exp_and_others"
SILU_TABLES = "silu_and_others"


class Signal:

    def __init__(self, sem, per_layer, start=0):
        self.sem, self.per_layer, self.start = sem, per_layer, start

    def at(self, layer, k):
        return layer * self.per_layer + (self.start + k)


def decoder_step(nc, x_prompt, x_sample, c_prompt, c_sample, cache_sb_k, cache_sb_v, state_gla,
                 page_table, cond_w, cond_b, norm_pre, norm_post, ffn_w_in, ffn_w_out, mix_w_in,
                 mix_w_out, gla_w_gate2, gla_b_gate, gla_norm, gm_ln_w, gm_ln_b, gm_ws, gm_bs,
                 sb_bias, y_prompt, y_sample, s_prompt, s_sample, k_prompt, v_prompt, k_sample,
                 v_sample, gm_v_sample):
    L, NPOOL, PAGE, SBH, HD = cache_sb_k.shape
    D = x_prompt.shape[2]
    NP = x_prompt.shape[1]
    B, TS = x_sample.shape[:2]
    NS = B * TS
    T = NP + NS
    KB = D // P
    KP = KB // 2
    FF = ffn_w_out.shape[2]
    FB = FF // P
    NC = 1 + B
    NPG = page_table.shape[1]
    GH = state_gla.shape[2]
    GW = GH * HD
    SBW = SBH * HD
    LR = gla_w_gate2.shape[1]
    TAU = 16.0
    GC = 64
    CPB = NP // GC
    PT_ = NP // P
    PR = SBH // 2
    GP = GH // 2
    SG = B // 4
    NOLD = NPG * PAGE
    NKEY = NOLD + NS
    assert (L, D, NP, NS, FB, NPG, PAGE, PR, GP, PT_) == (2, 1024, 256, 32, 22, 8, 128, 4, 2, 2)

    GQ, GK, GV, GG, MU, MV, SK, SQ, SV = 0, 2, 4, 6, 8, 10, 12, 16, 20
    NF = 24
    LRC = 4 * GW

    N_IN, N_OUT, N_MI, N_MO = FB, 2 * KB, NF // 2, KB // 2
    POS_IN = [0, N_IN + N_OUT + N_MI + N_MO]
    POS_OUT = [N_IN, POS_IN[1] + N_IN]
    POS_MI = N_IN + N_OUT
    POS_MO = POS_MI + N_MI
    NW = POS_OUT[1] + N_OUT
    NCH = 3 * D // 256
    NPC = B * NPG // 4
    DP_C = [2 * NCH + 2 * NPC, 0, NCH]
    DP_K = 2 * NCH
    DP_V = DP_K + NPC
    ND = 3 * NCH + 2 * NPC
    YB_OUT = [0, KB + 2 + N_MO + 2]
    YB_MO = KB + 2

    ctx = ExitStack()
    with ctx:
        sems = []

        def signal(name, per_layer=1, start=0):
            s = Signal(ctx.enter_context(nc.semaphore(name)), per_layer, start)
            sems.append(s)
            return s

        BASE = 16512
        TOP = 229344
        at = [BASE]

        def tile(name, shape, dt=F32, offset=None):
            words = int(np.prod(shape[1:]))
            here = at[0] if offset is None else offset
            t = nc.alloc_sbuf_tensor_at(name, shape, dt, offset=here)
            if offset is None:
                at[0] += -(-words * 4 // 32) * 32
            assert here + words * 4 <= TOP, (name, here, words)
            return t

        raw = tile("raw", [P, 2, 2048])
        w_hi = tile("w_hi", [P, 2, 2048], F32R)
        w_lo = tile("w_lo", [P, 2, 2048], F32R)
        direct = tile("direct", [P, 4, 2048])
        X = tile("X", [P, KB, T])
        y_region = at[0]
        Y = tile("Y", [P, KB, T])
        a_region = at[0]
        a_hi = tile("a_hi", [P, KB, T], F32R)
        a_lo = tile("a_lo", [P, KB, T], F32R)
        a_end = at[0]
        M = tile("M", [P, 3, NF, NC])
        cT = tile("cT", [P, KB, 32])
        vecs = tile("vecs", [P, L, P])
        vec = tile("vec", [P, P])
        V_CB, V_PRE, V_POST, V_GB, V_GN, V_LW, V_LB = 0, 72, 96, 120, 122, 124, 126
        rstd = tile("rstd", [P, 2, T])
        ident = tile("ident", [P, P])
        ones = tile("ones", [P, P])
        head_ones = tile("head_ones", [P, P])
        suffix = tile("suffix", [P, P])
        causal = tile("causal", [P, P])
        gla_mask = tile("gla_mask", [P, P])
        neg_mask = tile("neg_mask", [P, P])
        gla_mask_s = tile("gla_mask_s", [NS, NS])
        neg_mask_s = tile("neg_mask_s", [NS, NS])
        same_s = tile("same_s", [NS, B])
        rep = tile("rep", [TS, B, TS])
        restart = tile("restart", [P, T])
        pages = tile("pages", [1, B * NPG], I32)
        w2 = tile("w2", [LR, GW])
        sbb = tile("sbb", [P, SBH])
        sb_col = tile("sb_col", [SBH, 1])
        row_bias = tile("row_bias", [P, 1])
        row_head = tile("row_head", [SBH, PR, 4, 2, TS])
        new_mask = tile("new_mask", [P, SG, NS])
        lr = tile("lr", [LR, T])
        eps = tile("eps", [P, 1])
        shared = at[0]

        h_hi = tile("h_hi", [P, FB, T], F32R, shared)
        h_lo = tile("h_lo", [P, FB, T], F32R, shared + FB * T * 4)
        sg = tile("sg", [P, 2, T], F32, shared + 2 * FB * T * 4)
        hf = tile("hf", [P, 2, T], F32, shared + 2 * FB * T * 4 + 2 * T * 4)
        ysq = tile("ysq", [P, 4, T], F32, shared + 2 * FB * T * 4)
        crow = tile("crow", [P, NCH // 2 * P], F32, shared + (2 * FB + 4) * T * 4)
        row_query = tile("row_query", [NS, SG, PR, 4, 2, TS], F32, shared + (2 * FB + 4) * T * 4 + NCH // 2 * P * 4)
        xsq = tile("xsq", [P, KB, T], F32, shared)
        xtok = tile("xtok", [P, 3, D], F32, shared)
        ctok = tile("ctok", [NC, D], F32, shared + 3 * D * 4)
        vrow = tile("vrow", [P, L, P], F32, shared + 4 * D * 4)
        at[0] = shared
        Fm = tile("Fm", [P, NF, T])
        qz = tile("qz", [P, PR, 2, T])
        sv = tile("sv", [P, 3, SBW])
        g0 = at[0]
        gt = [tile(f"gt{i}", [P, GP, T]) for i in range(4)]
        gqz = tile("gqz", [P, GP, 2, T])
        gv = tile("gv", [P, 3, GW])
        kend = tile("kend", [P, CPB + 1, GW])
        att = tile("att", [P, PT_, GP, 2, P])
        att_s = tile("att_s", [NS, GP, 2, NS])
        S = tile("S", [P, 2, GP, P])
        S0 = tile("S0", [P, B, GP, HD])
        lr_raw = tile("lr_raw", [P, KB, LR], F32, g0 + 4 * 4 * GP * T - 4 * GP * T)
        assert at[0] <= TOP, at[0] - TOP
        lrw_hi = tile("lrw_hi", [P, KB, P], F32R, g0 + 4 * 4 * GP * T)
        lrw_lo = tile("lrw_lo", [P, KB, P], F32R, g0 + 4 * 4 * GP * T + KB * P * 4)
        z = tile("z", [P, SG, NKEY], F32, shared + SQ * T * 4)
        at[0] = g0
        sm = tile("sm", [P, SG, NKEY])
        sn = tile("sn", [P, SG, NKEY])
        a_rows = tile("a_rows", [P, NKEY])
        a_keys = tile("a_keys", [P, NPG, P])
        a_new = tile("a_new", [NS, P])
        o_rows = tile("o_rows", [P, 4, P])
        assert at[0] <= TOP, at[0] - TOP
        at[0] = a_region
        kst = tile("kst", [P, 3, SBW], F32, y_region)
        kt = tile("kt", [P, 2, 512])
        qd = tile("qd", [P, PR, 4, 4 * 2 * TS], F32, y_region + 3 * SBW * 4)
        vm = tile("vm", [NS, B, P], F32, at[0])
        dm = tile("dm", [P, GP, T])
        dsq = tile("dsq", [P, GP, T])
        vn = tile("vn", [P, 3, GW])
        wsr = tile("wsr", [P, GH, P])
        wst = tile("wst", [P, GH, P])
        wss = tile("wss", [NS, GH, NS])
        bs = tile("bs", [P, GP, P])
        assert at[0] <= a_end, at[0] - a_end
        zp0 = tile("zp0", [P, SBH, NP], F32, a_region)
        zp1 = tile("zp1", [P, SBH, P], F32, a_region + SBH * NP * 4)

        PS = ctx.enter_context(nc.psum_tensor("PS", [P, 8, 512], F32))

        raw_in = [[signal(f"raw_in{s}{h}", NW // 2) for h in range(2)] for s in range(2)]
        direct_in = [signal(f"direct_in{s}", ND // 4, NCH // 4) for s in range(4)]
        hi_done = signal("hi_done", 2 * NW)
        lo_done = signal("lo_done", 2 * NW, 4)
        w_used = signal("w_used", NW, 2)
        direct_used = signal("direct_used", ND, 4 + NCH)
        rows_in = signal("rows_in")
        small_in = signal("small_in")
        ws_in = signal("ws_in")
        s0_in = signal("s0_in")
        bs_in = signal("bs_in")
        const_ready = signal("const_ready")
        tposed = signal("tposed")
        start_copied = signal("start_copied")
        c_silu = signal("c_silu")
        cond_copied = signal("cond_copied", 3 * NCH // 2, 2 + NCH // 2)
        cond_t = signal("cond_t", 3, 1)
        mod_ready = signal("mod_ready", 3, 1)
        gu_free = signal("gu_free", 2 * (N_IN + 2))
        silu_done = signal("silu_done", 2 * N_IN)
        h_ready = signal("h_ready", 2 * N_IN)
        yb_free = signal("yb_free", 2 * (KB + 2) + (N_MO + 2))
        ssy_done = signal("ssy_done", 3)
        std_y = signal("std_y", 3)
        x_upd = signal("x_upd", 3 * KP)
        x_sq = signal("x_sq", 3 * KP, KP)
        x_scaled = signal("x_scaled", 3, 1)
        ssx_done = signal("ssx_done", 3, 1)
        std_x = signal("std_x", 3)
        a_f32 = signal("a_f32", 3 * KP)
        a_round = signal("a_round", 3 * KP)
        a_ready = signal("a_ready", 3 * KP)
        mix_evac = signal("mix_evac", N_MI + 2)
        zeroed = signal("zeroed", 2)
        lrw_round = signal("lrw_round")
        lrw_ready = signal("lrw_ready")
        pool_past = signal("pool_past", 7)
        outs_done = signal("outs_done")
        c_copied = signal("c_copied")
        lr_sum = signal("lr_sum")
        lr_ready = signal("lr_ready")
        gate_sum = signal("gate_sum")
        gate_n = signal("gate_n")
        gate_l = signal("gate_l")
        gate_b = signal("gate_b")
        gate_e = signal("gate_e")
        qz_ready = signal("qz_ready")
        kv_t = signal("kv_t", 6)
        kv_k = signal("kv_k", 3)
        kv_v = signal("kv_v", 3)
        row_set = signal("row_set")
        row_got = signal("row_got")
        mean_sum = signal("mean_sum")
        dev_ready = signal("dev_ready")
        var_sum = signal("var_sum")
        gm_std = signal("gm_std")
        vn_f = signal("vn_f")
        q_staged = signal("q_staged", SG)
        kt_t = signal("kt_t", B * NPG)
        kt_ready = signal("kt_ready", B * NPG)
        z_sum = signal("z_sum", SG)
        z_free = signal("z_free", SG + 1)
        gm_t = signal("gm_t", 4)
        gm_tc = signal("gm_tc", 4)
        wss_sum = signal("wss_sum")
        wss_ready = signal("wss_ready")
        gs_sum = signal("gs_sum", 3)
        gm_done = signal("gm_done")
        gla_in = signal("gla_in")
        gla_t = signal("gla_t", 3)
        gla_tc = signal("gla_tc", 3)
        att_sum = signal("att_sum", 3)
        att_ready = signal("att_ready", 3)
        s_sum = signal("s_sum", CPB)
        s_ready = signal("s_ready", CPB)
        vm_ready = signal("vm_ready", GP)
        ds_sum = signal("ds_sum", GP)
        s0_new = signal("s0_new", GP)
        o_sum = signal("o_sum", 3)
        o_sq = signal("o_sq")
        oss_sum = signal("oss_sum")
        o_std = signal("o_std")
        g_silu = signal("g_silu")
        gla_done = signal("gla_done")
        zp_sum = signal("zp_sum", PR)
        zp_evac = signal("zp_evac", PR)
        sp_n = signal("sp_n", 3)
        sp_l = signal("sp_l", 3)
        sp_ready = signal("sp_ready", 2)
        c_sum = signal("c_sum", 2)
        c_sub = signal("c_sub", 2)
        z_less = signal("z_less")
        A_ready = signal("A_ready", 2)
        staged = signal("staged", SG)
        a_turned = signal("a_turned", SG)
        a_copied = signal("a_copied", SG)
        o_rows_sum = signal("o_rows_sum", SG)
        o_rows_got = signal("o_rows_got", SG)
        o_turned = signal("o_turned", SG)
        bias_sum = signal("bias_sum")
        bias_got = signal("bias_got")
        op_sum = signal("op_sum", PR)
        op_evac = signal("op_evac", PR)
        heads_round = signal("heads_round")
        heads_ready = signal("heads_ready")
        out_t = signal("out_t")
        out_copied = signal("out_copied")
        k_out = signal("k_out")
        v_out = signal("v_out")
        gmv_out = signal("gmv_out")
        sp_out = signal("sp_out")
        ss_out = signal("ss_out")
        y_out = signal("y_out")
        
        ROWS = 3 + 7 * L + PT_ + 1

        block = ctx.enter_context(nc.Block())

        def halves(phase):
            return [(0, 768), (1024, 640)] if phase == "out" else [(0, 1024), (1024, 1024)]

        @block.sync
        def _(sp):
            def weights(l, pos, j, slot, parts):
                sp.wait_ge(lo_done.sem, lo_done.at(l, 2 * pos - 2) + 2 * j)
                for h, src in enumerate(parts):
                    n = src.shape[1] * src.shape[2]
                    dst = raw[:, slot, 1024 * h:1024 * h + n].rearrange("p (k c) -> p k c", c=P)
                    sp.dma_start(dst, src).then_inc(raw_in[slot][h].sem, 16)

            def ffn_in(l, n, j, slot, source=None):
                source = l if source is None else source
                cols = [ffn_w_in[source, n, :, ds(j * P + h * FF, P)] if not isinstance(j, int)
                        else ffn_w_in[source, n, :, j * P + h * FF:j * P + h * FF + P] for h in (0, 1)]
                weights(l, POS_IN[n], j, slot, [c.rearrange("(k p) c -> p k c", p=P) for c in cols])

            def ffn_out(l, n, m, part, slot, q):
                rows = [(11 * part, 6), (11 * part + 6, 5)]
                weights(l, POS_OUT[n], q, slot, [
                    ffn_w_out[l, n, r * P:(r + k) * P, ds(m * P, P)].rearrange("(k p) c -> p k c", p=P)
                    for r, k in rows])

            def mix(l, w, pos, j, slot, col):
                weights(l, pos, j, slot, [w[l, :, ds(col + h * P, P)].rearrange("(k p) c -> p k c", p=P)
                                          for h in (0, 1)])

            def room(l, dp, c):
                sp.wait_ge(direct_used.sem, direct_used.at(l, dp - 3) + c)

            def cond_load(lc, i, c, slot):
                for k in range(4):
                    r0 = (slot % 2) * (D // 2) + k * P
                    src = cond_w[lc, r0:r0 + P, ds(i * 3 * D + c * 1024 + (slot // 2) * 512, 512)]
                    sp.dma_start(direct[:, slot, 512 * k:512 * k + 512], src).then_inc(direct_in[slot].sem, 16)

            def cond(lc, l, i, c, slot):
                room(l, DP_C[i], c * 4 + slot)
                cond_load(lc, i, c, slot)

            def page_loop(l, cache, dp):
                with sp.Fori(0, NPC // 4) as i:
                    for q in range(4):
                        _, found = nc.values_load_multi_w_load_instructions(
                            pages[0:1, ds(i * 16 + 4 * q, 4)], engines=[sp.engine], min_val=0,
                            max_val=NPOOL - 1,
                            skip_runtime_bounds_check_because="the table holds the pool's page numbers")
                        room(l, dp, i * 4 + q)
                        for t, page in enumerate(found):
                            src = cache[l, ds(page, 1), :, :, :].rearrange("o s h d -> s (o h d)")
                            sp.dma_start(direct[:, q, 512 * t:512 * t + 512], src)\
                                .then_inc(direct_in[q].sem, 16)

            def ffn(l, n, conds_in, conds_out):
                with sp.Fori(0, NCH // 4) as i:
                    for s in range(4):
                        ffn_in(l, n, i * 4 + (s + 2), s % 2)
                        cond(*conds_in, i, s)
                with sp.Fori(NCH // 2 + 1, N_IN // 2) as i:
                    for s in range(2):
                        ffn_in(l, n, i * 2 + s, s)
                if conds_out:
                    with sp.Fori(0, NCH // 4) as i:
                        for s in range(4):
                            ffn_out(l, n, i * 2 + s // 2, s % 2, s % 2, i * 4 + s)
                            cond(*conds_out, i, s)
                    with sp.Fori(NCH // 4, N_OUT // 4) as i:
                        for s in range(4):
                            ffn_out(l, n, i * 2 + s // 2, s % 2, s % 2, i * 4 + s)
                else:
                    with sp.Fori(0, N_OUT // 4) as i:
                        for s in range(4):
                            ffn_out(l, n, i * 2 + s // 2, s % 2, s % 2, i * 4 + s)

            sp.dma_start(pages[:, :], page_table.rearrange("b n -> (b n)").unsqueeze(0)).then_inc(rows_in.sem, 16)
            sp.dma_start(ctok[0:1, :], c_prompt).then_inc(rows_in.sem, 16)
            sp.dma_start(ctok[1:NC, :], c_sample).then_inc(rows_in.sem, 16)
            for layer in range(L):
                for r, n, src in ((V_CB, 72, cond_b[layer].rearrange("(r p) -> r p", p=P)),
                                  (V_PRE, 24, norm_pre[layer].rearrange("i (r p) -> (i r) p", p=P)),
                                  (V_POST, 24, norm_post[layer].rearrange("i (r p) -> (i r) p", p=P)),
                                  (V_GB, 2, gla_b_gate[layer].rearrange("(r p) -> r p", p=P)),
                                  (V_GN, 2, gla_norm[layer].rearrange("(r p) -> r p", p=P)),
                                  (V_LW, 2, gm_ln_w[layer].rearrange("(r p) -> r p", p=P)),
                                  (V_LB, 2, gm_ln_b[layer].rearrange("(r p) -> r p", p=P))):
                    sp.dma_start(vrow[r:r + n, layer, :], src).then_inc(rows_in.sem, 16)
            for i in range(PT_):
                sp.dma_start(xtok[:, i, :], x_prompt[0, i * P:i * P + P, :]).then_inc(rows_in.sem, 16)
            sp.dma_start(xtok[0:NS, 2, :], x_sample.rearrange("b t d -> (b t) d")).then_inc(rows_in.sem, 16)
            for s in range(2):
                ffn_in(0, 0, s, s)
            with sp.Fori(0, NCH // 4) as i:
                for s in range(4):
                    sp.wait_ge(direct_used.sem, i * 4 + s + 1)
                    cond_load(0, 0, i, s)
            sp.wait_ge(rows_in.sem, ROWS * 16)

            with sp.Fori(0, L) as l:
                ffn(l, 0, (l, l, 1), (l, l, 2))
                with sp.Fori(0, LRC // 512) as i:
                    for s in range(2):
                        mix(l, mix_w_in, POS_MI, i * 2 + s, s, i * 512 + s * 256)
                for i, c in ((2, 2), (3, 4), (4, 3), (5, 5)):
                    for s in range(2):
                        mix(l, mix_w_in, POS_MI, i * 2 + s, s, c * 512 + s * 256 + LR)
                for s in range(2):
                    mix(l, mix_w_out, POS_MO, s, s, s * 256)
                page_loop(l, cache_sb_k, DP_K)
                page_loop(l, cache_sb_v, DP_V)
                for s in range(2):
                    mix(l, mix_w_out, POS_MO, 2 + s, s, (2 + s) * 256)
                for s in range(2):
                    ffn_in(l, 1, s, s)
                ffn(l, 1, (L - 1, l, 0), None)
                for s in range(2):
                    ffn_in(l + 1, 0, s, s, source=L - 1)
            sp.wait_ge(out_copied.sem, 1)
            for i in range(PT_):
                sp.dma_start(y_prompt[0, i * P:i * P + P, :], xtok[:, i, :]).then_inc(y_out.sem, 16)
            sp.dma_start(y_sample.rearrange("b t d -> (b t) d"), xtok[0:NS, 2, :]).then_inc(y_out.sem, 16)
            sp.wait_ge(y_out.sem, 48)

        @block.tensor
        def _(pe):
            def products(out, slot, word, src_hi, src_lo, k0, n, begins, ends):
                for i in range(n):
                    at_ = word + i * P
                    whi, wlo = w_hi[:, slot, at_:at_ + P], w_lo[:, slot, at_:at_ + P]
                    hi, lo = src_hi[:, k0 + i, :], src_lo[:, k0 + i, :]
                    pe.matmul(out, whi, hi, start=begins and i == 0, stop=False)
                    pe.matmul(out, whi, lo, start=False, stop=False)
                    last = pe.matmul(out, wlo, hi, start=False, stop=ends and i == n - 1)
                return last

            cond_sums = PS[:, 6:8, :].rearrange("p a b -> p (a b)")

            def cond_chunk(l, x, dp, c, slot):
                k = direct_in[slot]
                pair, half = divmod(slot, 2)
                if l is None:
                    pe.wait_ge(k.sem, c * 64 + 64)
                else:
                    pe.wait_ge(k.sem, k.at(l, dp // 4 + 1) * 64 + c * 64)
                if half == 0:
                    if l is None:
                        pe.wait_ge(cond_copied.sem, c * 2 + pair + 1)
                    else:
                        pe.wait_ge(cond_copied.sem, cond_copied.at(l, 6 * x - 1 + pair) + c * 2)
                for kb in range(4):
                    for g in range(4):
                        last = pe.matmul(PS[32 * g:32 * g + 32, 6 + pair, 0:P],
                                         cT[:, 4 * half + kb, :],
                                         direct[:, slot, kb * 512 + g * P:kb * 512 + g * P + P],
                                         start=half == 0 and kb == 0, stop=half == 1 and kb == 3)
                last.then_inc(direct_used.sem, 1)

            def cond_turn():
                for q in range(NCH // 2):
                    last = pe.transpose(cond_sums[:, q * P:q * P + P], crow[:, q * P:q * P + P], ident[:, :])
                last.then_inc(cond_t.sem, 1)

            def paired_products(s, banks, pair_ready):
                for k in range(KB):
                    if k % 2 == 0:
                        pair_ready(k // 2)
                    for h in range(2):
                        at_ = 1024 * h + k * P
                        whi, wlo = w_hi[:, s, at_:at_ + P], w_lo[:, s, at_:at_ + P]
                        out = PS[:, banks[h], 0:T]
                        pe.matmul(out, whi, a_hi[:, k, :], start=k == 0, stop=False)
                        pe.matmul(out, whi, a_lo[:, k, :], start=False, stop=False)
                        last = pe.matmul(out, wlo, a_hi[:, k, :], start=False, stop=k == KB - 1)
                return last

            def first_step(l, n, i):
                pos = POS_IN[n]
                pe.wait_ge(lo_done.sem, lo_done.at(l, 2 * pos + 2) + 8 * i)
                pe.wait_ge(gu_free.sem, gu_free.at(l, n * (N_IN + 2) + 1) + 4 * i)
                paired_products(0, (0, 2), lambda k: pe.wait_ge(a_ready.sem, a_ready.at(l, 2 * n * KP + k + 1)))\
                    .then_inc(w_used.sem, 1)

            def in_step(l, n, j, s):
                pos = POS_IN[n]
                par = s % 2
                for h in range(2):
                    pe.wait_ge(lo_done.sem, lo_done.at(l, 2 * pos + h + 1) + 2 * j)
                    if h == 0:
                        pe.wait_ge(gu_free.sem, gu_free.at(l, n * (N_IN + 2) + 1) + j)
                    last = products(PS[:, 2 * h + par, 0:T], par, 1024 * h, a_hi, a_lo, 0, KB, True, True)
                last.then_inc(w_used.sem, 1)

            def out_chunk(l, n, q, s):
                pos = POS_OUT[n]
                par, part, bank = s % 2, s % 2, (s // 2) % 2
                for h, (k, cnt) in enumerate(((0, 6), (6, 5))):
                    pe.wait_ge(lo_done.sem, lo_done.at(l, 2 * pos + h + 1) + 2 * q)
                    last = products(PS[:, bank, 0:T], par, 1024 * h, h_hi, h_lo, 11 * part + k, cnt,
                                    part == 0 and h == 0, part == 1 and h == 1)
                last.then_inc(w_used.sem, 1)

            def ffn(l, n, cond_in, cond_out):
                with pe.Fori(0, NCH // 4) as i:
                    for s in range(4):
                        if s == 0:
                            first_step(l, n, i)
                        else:
                            in_step(l, n, i * 4 + s, s)
                        if s == 0:
                            pe.wait_ge(mod_ready.sem, mod_ready.at(l, cond_in[0]))
                        cond_chunk(l, *cond_in, i, s)
                with pe.Fori(NCH // 2, NCH // 2 + 3) as i:
                    for s in range(2):
                        in_step(l, n, i * 2 + s, s)
                pe.wait_ge(cond_copied.sem, cond_copied.at(l, 6 * cond_in[0] + 6))
                cond_turn()
                with pe.Fori(NCH // 2 + 3, N_IN // 2) as i:
                    for s in range(2):
                        in_step(l, n, i * 2 + s, s)
                yb = YB_OUT[n]

                def squares(m, s, begins=False, ends=False):
                    pe.wait_ge(yb_free.sem, yb_free.at(l, yb + 3) + m)
                    return pe.matmul(PS[:, 5, 0:T], ones[:, :], ysq[:, s, :], start=begins, stop=ends)

                def group(i, with_cond, first=False, turn=False):
                    for s in range(4):
                        if s % 2 == 0:
                            pe.wait_ge(yb_free.sem, yb_free.at(l, yb + 1 + s // 2) + i * 2)
                        if first and s == 0:
                            pe.wait_ge(h_ready.sem, h_ready.at(l, n * N_IN + 11))
                        if first and s == 1:
                            pe.wait_ge(h_ready.sem, h_ready.at(l, (n + 1) * N_IN))
                        out_chunk(l, n, i * 4 + s, s)
                        if with_cond:
                            if s == 0:
                                pe.wait_ge(mod_ready.sem, mod_ready.at(l, cond_out[0]))
                            cond_chunk(l, *cond_out, i, s)
                        if s == 1 and turn:
                            pe.wait_ge(cond_copied.sem, cond_copied.at(l, 6 * cond_out[0] + 6))
                            cond_turn()
                        if s == 1 and not first:
                            squares(i * 2 - 1, 1)
                        if s == 3:
                            squares(i * 2, 0, begins=first)

                NG = N_OUT // 4
                group(0, bool(cond_out), True)
                if cond_out:
                    with pe.Fori(1, NG - 1) as i:
                        group(i, True)
                else:
                    with pe.Fori(1, NG - 1) as i:
                        group(i, False)
                group(NG - 1, False, turn=bool(cond_out))
                squares(2 * NG - 1, 1, ends=True).then_inc(ssy_done.sem, 1)

            def seam_squares(l, seam):
                for k in range(KB):
                    if k % 2 == 0:
                        pe.wait_ge(x_sq.sem, x_sq.at(l, seam * KP + k // 2 + 1))
                    last = pe.matmul(PS[:, 4, 0:T], ones[:, :], xsq[:, k, :], start=k == 0, stop=k == KB - 1)
                last.then_inc(ssx_done.sem, 1)

            def token_tile(i):
                return (slice(i * P, i * P + P), P) if i < PT_ else (slice(NP, T), NS)

            pe.wait_ge(const_ready.sem, 1)
            pe.wait_ge(c_silu.sem, 1)
            for k in range(KB):
                pe.transpose(PS[:, 0, k * NC:k * NC + NC], ctok[:, k * P:k * P + P], ident[0:NC, 0:NC])
            pe.wait_ge(rows_in.sem, ROWS * 16)
            for layer in range(L):
                pe.transpose(PS[:, 1, layer * P:layer * P + P], vrow[:, layer, :], ident[:, :])
            for i in range(3):
                sl, n = token_tile(i)
                for k in range(KB):
                    last = pe.transpose(PS[:, 2 + 2 * i + k // 4,
                                           (k % 4) * P:(k % 4) * P + n],
                                        xtok[0:n, i, k * P:k * P + P], ident[0:n, 0:n])
            last.then_inc(tposed.sem, 1)
            pe.wait_ge(c_copied.sem, 1)
            pe.wait_ge(start_copied.sem, 1)
            for g in range(SG):
                last = pe.matmul(PS[:, 2, g * NS:g * NS + NS],
                                 row_query[:, g, :, :, :, :].rearrange("k a b c d -> k (a b c d)"),
                                 neg_mask_s[:, :], start=True, stop=True)
            last.then_inc(row_set.sem, 1)
            for k in range(KB):
                pe.wait_ge(x_sq.sem, k // 2 + 1)
                last = pe.matmul(PS[:, 4, 0:T], ones[:, :], xsq[:, k, :], start=k == 0, stop=k == KB - 1)
            last.then_inc(ssx_done.sem, 1)
            with pe.Fori(0, NCH // 4) as i:
                for s in range(4):
                    cond_chunk(None, 0, 0, i, s)
            pe.wait_ge(cond_copied.sem, 8)
            cond_turn()

            with pe.Fori(0, L) as l:
                ffn(l, 0, (0, DP_C[1]), (1, DP_C[2]))
                seam_squares(l, 0)

                with pe.Fori(0, N_MI // 2) as i:
                    for s in range(2):
                        if s == 0:
                            pe.wait_ge(lo_done.sem, lo_done.at(l, 2 * POS_MI + 2) + 4 * i)
                            pe.wait_ge(mix_evac.sem, mix_evac.at(l, 1) + 2 * i)
                            last = paired_products(0, (0, 1), lambda k: pe.wait_ge(
                                a_ready.sem, a_ready.at(l, KP + k + 1)))
                        else:
                            for h in range(2):
                                pe.wait_ge(lo_done.sem, lo_done.at(l, 2 * POS_MI + h + 3) + 4 * i)
                                if h == 0:
                                    pe.wait_ge(mix_evac.sem, mix_evac.at(l, 2) + 2 * i)
                                last = products(PS[:, 2 + h, 0:T], 1, 1024 * h, a_hi, a_lo, 0, KB, True, True)
                        last.then_inc(w_used.sem, 1)
                pe.wait_ge(lrw_ready.sem, lrw_ready.at(l, 1))
                for k in range(KB):
                    pe.matmul(PS[:, 7, 0:T], lrw_hi[:, k, :], a_hi[:, k, :], start=k == 0, stop=False)
                    pe.matmul(PS[:, 7, 0:T], lrw_hi[:, k, :], a_lo[:, k, :], start=False, stop=False)
                    last = pe.matmul(PS[:, 7, 0:T], lrw_lo[:, k, :], a_hi[:, k, :], start=False, stop=k == KB - 1)
                last.then_inc(lr_sum.sem, 1)

                pe.wait_ge(mix_evac.sem, mix_evac.at(l, N_MI + 2))
                for j in range(GP):
                    last = pe.matmul(PS[:, 6, 0:T], ones[:, :], Fm[:, MV + j, :], start=j == 0, stop=j == GP - 1)
                last.then_inc(mean_sum.sem, 1)
                pe.wait_ge(lr_ready.sem, lr_ready.at(l, 1))
                for j in range(GP):
                    last = pe.matmul(PS[:, 4 + j, 0:T], w2[:, j * P:j * P + P], lr[:, :], start=True, stop=True)
                last.then_inc(gate_sum.sem, 1)
                for i in range(3):
                    sl, n = token_tile(i)
                    for which, f0 in ((0, SK), (1, SV)):
                        bank = 2 + which
                        if i:
                            done = (kv_k, kv_v)[which]
                            pe.wait_ge(done.sem, done.at(l, i))
                        for p in range(PR):
                            last = pe.transpose(PS[0:n, bank, p * P:p * P + P], Fm[:, f0 + p, sl], ident[:, :])
                        last.then_inc(kv_t.sem, 1)
                pe.wait_ge(dev_ready.sem, dev_ready.at(l, 1))
                for j in range(GP):
                    last = pe.matmul(PS[:, 6, 0:T], ones[:, :], dsq[:, j, :], start=j == 0, stop=j == GP - 1)
                last.then_inc(var_sum.sem, 1)
                pe.wait_ge(small_in.sem, small_in.at(l, 1) * 64)
                pe.wait_ge(gm_std.sem, gm_std.at(l, 1))
                pe.matmul(PS[:, 6, 0:1], row_head[:, :, :, :, :].rearrange("k a b c d -> k (a b c d)"),
                          sb_col[:, :], start=True, stop=True).then_inc(bias_sum.sem, 1)

                with pe.Fori(0, SG) as i:
                    def turn(n):
                        q, t = divmod(n, 4)
                        if t == 0:
                            k = direct_in[q % 4]
                            pe.wait_ge(k.sem, k.at(l, DP_K // 4 + 1 + q // 4) * 64 + 128 * i)
                        for p in range(PR):
                            last = pe.transpose(PS[:, 6 + n % 2, p * P:p * P + P],
                                                direct[:, q % 4, 512 * t + p * P:512 * t + p * P + P], ident[:, :])
                        last.then_inc(kt_t.sem, 1)

                    def score(n):
                        pe.wait_ge(kt_ready.sem, kt_ready.at(l, n + 1) + 4 * NPG * i)
                        smp, page = divmod(n, NPG)
                        for p in range(PR):
                            last = pe.matmul(PS[32 * p:32 * p + 32, page // 4, page % 4 * P:page % 4 * P + P],
                                             qd[:, p, smp, :], kt[:, n % 2, p * P:p * P + P],
                                             start=smp == 0 and page % 4 == 0, stop=smp == 3 and page % 4 == 3)
                        if n % 4 == 3:
                            last.then_inc(direct_used.sem, 1)

                    pe.wait_ge(bias_got.sem, bias_got.at(l, 1))
                    turn(0)
                    pe.wait_ge(q_staged.sem, q_staged.at(l, 1) + i)
                    pe.wait_ge(z_free.sem, z_free.at(l, 1) + i)
                    for n in range(4 * NPG):
                        if n + 1 < 4 * NPG:
                            turn(n + 1)
                        score(n)
                    for p in range(PR):
                        for smp in range(4):
                            last = pe.matmul(PS[32 * p:32 * p + 32, 2, 0:NS], qd[:, p, smp, :], Fm[:, SK + p, NP:T],
                                             start=smp == 0, stop=smp == 3)
                    last.then_inc(z_sum.sem, 1)

                for h in range(GH):
                    if h == 0:
                        pe.wait_ge(ws_in.sem, ws_in.at(l, 1) * 16)
                        pe.wait_ge(kv_v.sem, kv_v.at(l, 3))
                    last = pe.transpose(PS[:, 3, h * P:h * P + P], wsr[:, h, :], ident[:, :])
                last.then_inc(gm_t.sem, 1)
                pe.wait_ge(vn_f.sem, vn_f.at(l, 1))
                pe.wait_ge(gm_tc.sem, gm_tc.at(l, 1))
                for i in range(3):
                    sl, n = token_tile(i)
                    bank = 1 + i % 2
                    if i == 0:
                        pe.wait_ge(z_free.sem, z_free.at(l, SG + 1))
                        pe.wait_ge(kv_k.sem, kv_k.at(l, 3))
                    if i == 2:
                        pe.wait_ge(gm_tc.sem, gm_tc.at(l, 2))
                    for j in range(GP):
                        last = pe.transpose(PS[0:n, bank, j * P:j * P + P], dm[:, j, sl], ident[:, :])
                    last.then_inc(gm_t.sem, 1)
                pe.matmul(PS[0:NS, 4, 0:GH * TS], rep[:, :, :].rearrange("s b t -> s (b t)"),
                          wst[0:TS, :, 0:TS], start=True, stop=True).then_inc(wss_sum.sem, 1)
                pe.wait_ge(gm_tc.sem, gm_tc.at(l, 4))
                for i in range(PT_):
                    for j in range(GP):
                        last = pe.matmul(PS[:, 1 + i, 256 * j:256 * j + 256], vn[:, i, j * P:j * P + P],
                                         wst[:, 2 * j:2 * j + 2, :], start=True, stop=True)
                    last.then_inc(gs_sum.sem, 1)
                pe.wait_ge(wss_ready.sem, wss_ready.at(l, 1))
                for j in range(GP):
                    last = pe.matmul(PS[:, 3, 64 * j:64 * j + 64], vn[0:NS, 2, j * P:j * P + P],
                                     wss[:, 2 * j:2 * j + 2, :], start=True, stop=True)
                last.then_inc(gs_sum.sem, 1)

                pe.wait_ge(gla_in.sem, gla_in.at(l, 1))
                for i in range(3):
                    sl, n = token_tile(i)
                    if i == 2:
                        pe.wait_ge(gla_tc.sem, gla_tc.at(l, 1))
                    for j in range(GP):
                        pe.transpose(PS[0:n, 6 + i % 2, j * P:j * P + P], Fm[:, GV + j, sl], ident[:, :])
                    for j in range(GP):
                        last = pe.transpose(PS[0:n, 6 + i % 2, 256 + j * P:256 + j * P + P], gt[3][:, j, sl], ident[:, :])
                    last.then_inc(gla_t.sem, 1)
                for i in range(3):
                    sl, n = token_tile(i)
                    bank = (4, 5, 0)[i]
                    if i == 0:
                        pe.wait_ge(wss_ready.sem, wss_ready.at(l, 1))
                    for j in range(GP):
                        last = pe.matmul(PS[0:n, bank, 2 * n * j:2 * n * j + 2 * n], gt[0][:, j, sl],
                                         gqz[:, j, :, sl], start=True, stop=True)
                    last.then_inc(att_sum.sem, 1)
                pe.wait_ge(gm_done.sem, gm_done.at(l, 1))
                pe.wait_ge(gla_tc.sem, gla_tc.at(l, 3))
                for i in range(PT_):
                    pe.wait_ge(att_ready.sem, att_ready.at(l, i + 1))
                    for j in range(GP):
                        last = pe.matmul(PS[:, 1 + i, 256 * j:256 * j + 256], gv[:, i, j * P:j * P + P],
                                         att[:, i, j, :, :], start=j == 0, stop=False)
                    for cc in range(2):
                        c = 2 * i + cc
                        if c:
                            pe.wait_ge(s_ready.sem, s_ready.at(l, c))
                            for j in range(GP):
                                out = PS[:, 1 + i, 256 * j:256 * j + 256].rearrange("p (h t) -> p h t", h=2)
                                last = pe.matmul(out[:, :, cc * GC:cc * GC + GC], S[:, (c - 1) % 2, j, :],
                                                 gqz[:, j, :, c * GC:c * GC + GC], start=False,
                                                 stop=cc == 1 and j == GP - 1)
                        if cc == 1:
                            last.then_inc(o_sum.sem, 1)
                        for j in range(GP):
                            last = pe.matmul(PS[:, 6 + c % 2, j * P:j * P + P], kend[:, c, j * P:j * P + P],
                                             gv[:, i, j * P:j * P + P], start=True, stop=True)
                        last.then_inc(s_sum.sem, 1)
                pe.wait_ge(att_ready.sem, att_ready.at(l, 3))
                pe.wait_ge(s0_in.sem, s0_in.at(l, 1) * 32)
                for j in range(GP):
                    pe.matmul(PS[:, 3, 64 * j:64 * j + 64], gv[0:NS, 2, j * P:j * P + P],
                              att_s[:, j, :, :], start=j == 0, stop=False)
                for j in range(GP):
                    for h in range(2):
                        for b in range(B):
                            at_ = 64 * j + 32 * h + TS * b
                            last = pe.matmul(PS[64 * h:64 * h + 64, 3, at_:at_ + TS], S0[:, b, j, :],
                                             gqz[:, j, h, NP + TS * b:NP + TS * b + TS],
                                             start=False, stop=j == GP - 1 and b == B - 1)
                last.then_inc(o_sum.sem, 1)
                for j in range(GP):
                    pe.wait_ge(vm_ready.sem, vm_ready.at(l, j + 1))
                    if j:
                        pe.wait_ge(s0_new.sem, s0_new.at(l, 1))
                    for q in range(2):
                        last = pe.matmul(PS[:, 4 + q, :], kend[0:NS, CPB, j * P:j * P + P],
                                         vm[:, 4 * q:4 * q + 4, :], start=True, stop=True)
                    last.then_inc(ds_sum.sem, 1)
                pe.wait_ge(o_sq.sem, o_sq.at(l, 1))
                pe.wait_ge(s_ready.sem, s_ready.at(l, CPB))
                for j in range(GP):
                    last = pe.matmul(PS[:, 6 + j, 0:T], head_ones[:, :], gt[2][:, j, :], start=True, stop=True)
                last.then_inc(oss_sum.sem, 1)

                pe.wait_ge(gla_done.sem, gla_done.at(l, 1))
                for p in range(PR):
                    if p:
                        pe.wait_ge(zp_evac.sem, zp_evac.at(l, p))
                    pe.matmul(PS[:, 6, :], Fm[:, SK + p, 0:P], qz[:, p, :, 0:NP], start=True, stop=True)
                    pe.matmul(PS[:, 7, 0:256], Fm[:, SK + p, P:NP], qz[:, p, :, P:NP], start=True, stop=True)\
                        .then_inc(zp_sum.sem, 1)
                for g in range(2):
                    pe.wait_ge(sp_ready.sem, sp_ready.at(l, 1 + g))
                    if g == 0:
                        pe.wait_ge(zp_evac.sem, zp_evac.at(l, PR))
                    else:
                        pe.wait_ge(c_sub.sem, c_sub.at(l, 1))
                    snf = sn[:, :, :].rearrange("p a b -> p (a b)")
                    for p in range(2):
                        top = snf[:, 512 * p:512 * p + 512]
                        low = snf[:, 1024 + 256 * p:1024 + 256 * p + 256]
                        pe.matmul(PS[:, p, :], suffix[:, :], top, start=True, stop=False)
                        pe.matmul(PS[:, p, :].rearrange("p (h q) -> p h q", h=2)[:, :, P:NP], ones[:, :],
                                  low, start=False, stop=True)
                        last = pe.matmul(PS[:, 2, 256 * p:256 * p + 256], suffix[:, :], low, start=True, stop=True)
                    last.then_inc(c_sum.sem, 1)
                for p in range(PR):
                    if p == 0:
                        pe.wait_ge(A_ready.sem, A_ready.at(l, 1))
                        pe.wait_ge(kv_v.sem, kv_v.at(l, 3))
                    if p == 2:
                        pe.wait_ge(A_ready.sem, A_ready.at(l, 2))
                    if p >= 2:
                        pe.wait_ge(op_evac.sem, op_evac.at(l, p - 1))
                    pe.matmul(PS[:, 6 + p % 2, :], sv[:, 0, p * P:p * P + P], zp0[:, 2 * p:2 * p + 2, :],
                              start=True, stop=False)
                    pe.matmul(PS[:, 6 + p % 2, :].rearrange("p (h q) -> p h q", h=2)[:, :, P:NP],
                              sv[:, 1, p * P:p * P + P], zp1[:, 2 * p:2 * p + 2, :],
                              start=False, stop=True).then_inc(op_sum.sem, 1)
                with pe.Fori(0, SG) as i:
                    pe.wait_ge(staged.sem, staged.at(l, 1) + i)
                    for page in range(NPG):
                        pe.transpose(PS[:, page // 4, page % 4 * P:page % 4 * P + P],
                                     a_rows[:, page * P:page * P + P], ident[:, :])
                    pe.transpose(PS[0:NS, 2, 0:P], a_rows[:, NOLD:NKEY], ident[:, :]).then_inc(a_turned.sem, 1)
                    pe.wait_ge(a_copied.sem, a_copied.at(l, 1) + i)
                    for smp in range(4):
                        for q in range(2):
                            slot = (2 * smp + q) % 4
                            k = direct_in[slot]
                            pe.wait_ge(k.sem, k.at(l, DP_V // 4 + 1 + smp // 2) * 64 + 128 * i)
                            for t in range(4):
                                page = 4 * q + t
                                for p in range(PR):
                                    last = pe.matmul(PS[32 * p:32 * p + 32, 4, smp * P:smp * P + P],
                                                     a_keys[:, page, 32 * p:32 * p + 32],
                                                     direct[:, slot, 512 * t + p * P:512 * t + p * P + P],
                                                     start=smp == 0 and page == 0, stop=False)
                            last.then_inc(direct_used.sem, 1)
                    for p in range(PR):
                        for smp in range(4):
                            last = pe.matmul(PS[32 * p:32 * p + 32, 4, smp * P:smp * P + P],
                                             a_new[:, 32 * p:32 * p + 32], sv[0:NS, 2, p * P:p * P + P],
                                             start=False, stop=smp == 3)
                    last.then_inc(o_rows_sum.sem, 1)
                    pe.wait_ge(o_rows_got.sem, o_rows_got.at(l, 1) + i)
                    for smp in range(4):
                        last = pe.transpose(PS[:, 5, smp * P:smp * P + P], o_rows[:, smp, :], ident[:, :])
                    last.then_inc(o_turned.sem, 1)

                pe.wait_ge(heads_ready.sem, heads_ready.at(l, 1))
                for j in range(N_MO):
                    s = j % 2
                    for h in range(2):
                        pe.wait_ge(lo_done.sem, lo_done.at(l, 2 * (POS_MO + j) + h + 1))
                        if h == 0:
                            pe.wait_ge(yb_free.sem, yb_free.at(l, KB + 2 + j + 1))
                        last = products(PS[:, 2 * s + h, 0:T], s, 1024 * h, a_hi, a_lo, 0, KB, True, True)
                    last.then_inc(w_used.sem, 1)
                    if j:
                        pe.wait_ge(yb_free.sem, yb_free.at(l, KB + 2 + 2 + j))
                        for h in range(2):
                            last = pe.matmul(PS[:, 5, 0:T], ones[:, :], ysq[:, 2 * ((j - 1) % 2) + h, :], start=j == 1 and h == 0, stop=False)
                pe.wait_ge(yb_free.sem, yb_free.at(l, KB + 2 + 2 + N_MO))
                for h in range(2):
                    last = pe.matmul(PS[:, 5, 0:T], ones[:, :], ysq[:, 2 * ((N_MO - 1) % 2) + h, :], start=False, stop=h == 1)
                last.then_inc(ssy_done.sem, 1)
                seam_squares(l, 1)
                ffn(l, 1, (2, DP_C[0]), None)
                seam_squares(l, 2)
            pe.wait_ge(x_upd.sem, x_upd.at(L, 0))
            for i in range(3):
                sl, n = token_tile(i)
                for k in range(KB):
                    bank = 2 * i + k // 4
                    last = pe.transpose(PS[0:n, bank, (k % 4) * P:(k % 4) * P + P], X[:, k, sl], ident[:, :])
            last.then_inc(out_t.sem, 1)


        @block.scalar
        def _(act):
            def split(l, pos, i, s, kind="in"):
                for h, (at_, n) in enumerate(halves(kind)):
                    k = raw_in[s][h]
                    act.wait_ge(k.sem, k.at(l, pos // 2 + 1) * 16 + i * 16)
                    if h == 0:
                        act.wait_ge(w_used.sem, w_used.at(l, pos + s - 1) + 2 * i)
                    act.activation(w_hi[:, s, at_:at_ + n], raw[:, s, at_:at_ + n], ACT.Copy)\
                        .then_inc(hi_done.sem, 1)

            def ffn(l, n, after):
                pos, out = POS_IN[n], POS_OUT[n]

                def silu(j, s):
                    act.wait_ge(w_used.sem, w_used.at(l, pos + 1) + j)
                    act.wait_ge(gu_free.sem, gu_free.at(l, n * (N_IN + 2) + 1) + j)
                    act.activation(sg[:, s, :], PS[:, s, 0:T], ACT.Silu).then_inc(silu_done.sem, 1)

                act.preload_act_table_set(SILU_TABLES)
                with act.Fori(0, N_IN // 2 - 1) as i:
                    for s in range(2):
                        split(l, pos, i + 1, s)
                        silu(i * 2 + s, s)
                for s in range(2):
                    split(l, out, 0, s, "out")
                    silu(N_IN - 2 + s, s)
                act.drain()
                act.sem_inc(yb_free.sem, 2)
                act.preload_act_table_set(LOG_TABLES)

                def evac(m, s):
                    act.wait_ge(w_used.sem, w_used.at(l, out + 2) + 2 * m)
                    act.activation(Y[:, ds(m, 1), :] if not isinstance(m, int) else Y[:, m:m + 1, :],
                                   PS[:, s:s + 1, 0:T], ACT.Copy)
                    act.activation(ysq[:, s, :], PS[:, s, 0:T], ACT.Square).then_inc(yb_free.sem, 1)

                with act.Fori(0, KB // 2 - 1) as i:
                    for g in range(2):
                        for s in range(2):
                            split(l, out, 2 * i + 1 + g, s, "out")
                        evac(2 * i + g, g)
                for s in range(2):
                    split(l, out, KB - 1, s, "out")
                evac(KB - 2, 0)
                split(*after, 0, 0)
                evac(KB - 1, 1)
                split(*after, 0, 1)

            def rsqrt(out, mean, scale):
                act.activation(out, mean, ACT.Ln, scale=scale, bias=eps[:, :])
                act.drain()
                return act.activation(out, out, ACT.Exp, scale=-0.5)

            def scale_prompt(p, pair):
                for kb in (2 * pair, 2 * pair + 1):
                    last = act.activation(Y[:, kb, 0:NP], X[:, kb, 0:NP], ACT.Copy, scale=M[:, p, KB + kb, 0:1])
                return last

            def seam_post(l, k):
                act.wait_ge(ssy_done.sem, ssy_done.at(l, k + 1))
                rsqrt(rstd[:, 0, :], PS[:, 5, 0:T], 1.0 / D).then_inc(std_y.sem, 1)
                for j in range(KP):
                    act.wait_ge(x_upd.sem, x_upd.at(l, k * KP + j + 1))
                    act.activation(xsq[:, 2 * j:2 * j + 2, :], X[:, 2 * j:2 * j + 2, :], ACT.Square)\
                        .then_inc(x_sq.sem, 1)
                    last = scale_prompt((k + 1) % 3, j)
                last.then_inc(x_scaled.sem, 1)

            def pre(l, p):
                act.wait_ge(ssx_done.sem, ssx_done.at(l, p))
                rsqrt(rstd[:, 1, :], PS[:, 4, 0:T], 1.0 / D).then_inc(std_x.sem, 1)
                for j in range(KP):
                    act.wait_ge(a_f32.sem, a_f32.at(l, p * KP + j + 1))
                    for kb in (2 * j, 2 * j + 1):
                        act.activation(a_hi[:, kb, 0:NP], Y[:, kb, 0:NP], ACT.Identity, bias=M[:, p, kb, 0:1])
                    act.activation(a_hi[:, 2 * j:2 * j + 2, NP:T], Y[:, 2 * j:2 * j + 2, NP:T], ACT.Copy)\
                        .then_inc(a_round.sem, 1)

            act.wait_ge(rows_in.sem, ROWS * 16)
            act.activation(ctok[:, :], ctok[:, :], ACT.Silu).then_inc(c_silu.sem, 1)
            act.wait_ge(tposed.sem, 1)
            act.activation(cT[:, :, 0:NC], PS[:, 0, 0:KB * NC].rearrange("p (k c) -> p k c", c=NC), ACT.Copy)
            act.activation(vecs[:, :, :], PS[:, 1, 0:L * P].rearrange("p (k c) -> p k c", c=P), ACT.Copy)\
                .then_inc(c_copied.sem, 1)
            act.wait_ge(start_copied.sem, 1)
            for j in range(KP):
                act.activation(xsq[:, 2 * j:2 * j + 2, :], X[:, 2 * j:2 * j + 2, :], ACT.Square)\
                    .then_inc(x_sq.sem, 1)
            act.preload_act_table_set(LOG_TABLES)
            for s in range(2):
                split(0, POS_IN[0], 0, s)
            act.wait_ge(mod_ready.sem, 1)
            for j in range(KP):
                last = scale_prompt(0, j)
            last.then_inc(x_scaled.sem, 1)

            with act.Fori(0, L) as l:
                pre(l, 0)
                ffn(l, 0, (l, POS_MI))
                seam_post(l, 0)
                pre(l, 1)

                act.wait_ge(small_in.sem, small_in.at(l, 1) * 64)
                act.wait_ge(zeroed.sem, zeroed.at(l, 1))
                act.activation(lrw_hi[:, :, 0:LR], lr_raw[:, :, :], ACT.Copy).then_inc(lrw_round.sem, 1)
                act.sem_inc(mix_evac.sem, 2)

                def mix_read(j, s):
                    act.wait_ge(w_used.sem, w_used.at(l, POS_MI + 1) + j)
                    out = Fm[:, 2 * j:2 * j + 2, :] if isinstance(j, int) else Fm[:, ds(2 * j, 2), :]
                    act.activation(out, PS[:, 2 * s:2 * s + 2, 0:T], ACT.Copy).then_inc(mix_evac.sem, 1)

                with act.Fori(0, N_MI // 2 - 1) as i:
                    for s in range(2):
                        split(l, POS_MI, i + 1, s)
                        mix_read(i * 2 + s, s)
                for s in range(2):
                    split(l, POS_MO, 0, s)
                    mix_read(N_MI - 2 + s, s)
                act.wait_ge(lr_sum.sem, lr_sum.at(l, 1))
                act.activation(lr[:, :], PS[0:LR, 7, 0:T], ACT.Copy).then_inc(lr_ready.sem, 1)
                for i in range(3):
                    n = P if i < PT_ else NS
                    act.wait_ge(kv_t.sem, kv_t.at(l, 2 * i + 1))
                    act.activation(kst[0:n, i, :], PS[0:n, 2, :], ACT.Copy).then_inc(kv_k.sem, 1)
                act.wait_ge(var_sum.sem, var_sum.at(l, 1))
                rsqrt(rstd[:, 0, :], PS[:, 6, 0:T], 1.0 / GW).then_inc(gm_std.sem, 1)
                act.wait_ge(gate_n.sem, gate_n.at(l, 1))
                act.activation(gt[1][:, :, :], gt[1][:, :, :], ACT.Exp)
                act.drain()
                act.activation(gt[1][:, :, :], gt[1][:, :, :], ACT.Ln, bias=1.0).then_inc(gate_l.sem, 1)
                act.wait_ge(gate_b.sem, gate_b.at(l, 1))
                act.activation(gt[3][:, :, :], gt[3][:, :, :], ACT.Exp, scale=1.0 / TAU)
                act.activation(gt[0][:, :, :], gt[2][:, :, :], ACT.Exp, scale=-1.0 / TAU)
                act.activation(gt[1][:, :, :], gt[2][:, :, :], ACT.Exp, scale=1.0 / TAU).then_inc(gate_e.sem, 1)

                act.wait_ge(qz_ready.sem, qz_ready.at(l, 1))
                act.wait_ge(kv_t.sem, kv_t.at(l, 6))
                act.sem_inc(z_free.sem, 1)
                act.wait_ge(bias_sum.sem, bias_sum.at(l, 1))
                act.activation(row_bias[:, :], PS[:, 6, 0:1], ACT.Copy).then_inc(bias_got.sem, 1)
                act.drain()
                act.wait_ge(zeroed.sem, zeroed.at(l, 2))
                with act.Fori(0, SG) as i:
                    for smp in range(4):
                        out = qd[:, :, smp, 8 * smp:8 * smp + 8].rearrange("d p (h t) -> d p h t", h=2)
                        last = act.activation(out, qz[:, :, :, ds(i * 4 * TS + (NP + TS * smp), TS)], ACT.Copy)
                    last.then_inc(q_staged.sem, 1)
                    for n in range(4 * NPG):
                        act.wait_ge(kt_t.sem, kt_t.at(l, n + 1) + 4 * NPG * i)
                        act.activation(kt[:, n % 2, :], PS[:, 6 + n % 2, :], ACT.Copy)\
                            .then_inc(kt_ready.sem, 1)
                    act.wait_ge(z_sum.sem, z_sum.at(l, 1) + i)
                    act.activation(z[:, ds(i, 1), 0:NOLD], PS[:, 0:2, :].rearrange("p a b -> p (a b)").unsqueeze(1),
                                   ACT.Identity, scale=HD ** -0.5, bias=row_bias[:, :])
                    act.activation(z[:, ds(i, 1), NOLD:], PS[:, 2:3, 0:NS], ACT.Identity,
                                   scale=HD ** -0.5, bias=row_bias[:, :]).then_inc(z_free.sem, 1)

                act.activation(Fm[:, GG:GG + 2, :], Fm[:, GG:GG + 2, :], ACT.Silu).then_inc(g_silu.sem, 1)
                act.preload_act_table_set(LOG_TABLES)
                act.wait_ge(oss_sum.sem, oss_sum.at(l, 1))
                rsqrt(gt[2][:, :, :], PS[:, 6:8, 0:T], 1.0 / HD).then_inc(o_std.sem, 1)


                def log1p_exp(k, parts):
                    act.wait_ge(sp_n.sem, sp_n.at(l, k))
                    for a in parts:
                        act.activation(a, a, ACT.Exp)
                    act.drain()
                    for i, a in enumerate(parts):
                        last = act.activation(a, a, ACT.Ln, bias=1.0)
                    last.then_inc(sp_l.sem, 1)

                log1p_exp(1, [sm[:, :, :]])
                act.wait_ge(gmv_out.sem, gmv_out.at(l, 1) * 16)
                for p in range(PR):
                    act.wait_ge(zp_sum.sem, zp_sum.at(l, p + 1))
                    for h in range(2):
                        b_ = sbb[:, 2 * p + h:2 * p + h + 1]
                        act.activation(zp0[:, 2 * p + h, :], PS[:, 6, NP * h:NP * h + NP], ACT.Identity,
                                       scale=HD ** -0.5, bias=b_)
                        last = act.activation(zp1[:, 2 * p + h, :], PS[:, 7, P * h:P * h + P], ACT.Identity,
                                              scale=HD ** -0.5, bias=b_)
                    last.then_inc(zp_evac.sem, 1)
                for g in range(2):
                    log1p_exp(2 + g, [sn[:, :, :].rearrange("p a b -> p (a b)")[:, 0:1536]])
                    act.wait_ge(c_sub.sem, c_sub.at(l, 1 + g))
                    act.activation(zp0[:, 4 * g:4 * g + 4, :], zp0[:, 4 * g:4 * g + 4, :], ACT.Exp)
                    act.activation(zp1[:, 4 * g:4 * g + 4, :], zp1[:, 4 * g:4 * g + 4, :], ACT.Exp)\
                        .then_inc(A_ready.sem, 1)
                act.drain()
                act.wait_ge(k_out.sem, k_out.at(l, 1) * 48)
                act.wait_ge(sp_out.sem, sp_out.at(l, 1) * 32)
                act.wait_ge(z_less.sem, z_less.at(l, 1))
                with act.Fori(0, SG) as i:
                    act.activation(a_rows[:, :].unsqueeze(1), z[:, ds(i, 1), :], ACT.Exp).then_inc(staged.sem, 1)
                    act.wait_ge(a_turned.sem, a_turned.at(l, 1) + i)
                    act.activation(a_keys[:, :, :], PS[:, 0:2, :].rearrange("p a (b c) -> p (a b) c", c=P), ACT.Copy)
                    act.activation(a_new[:, :], PS[0:NS, 2, 0:P], ACT.Copy).then_inc(a_copied.sem, 1)
                    act.wait_ge(o_rows_sum.sem, o_rows_sum.at(l, 1) + i)
                    act.activation(o_rows[:, :, :], PS[:, 4, :].rearrange("p (a b) -> p a b", a=4), ACT.Copy)\
                        .then_inc(o_rows_got.sem, 1)
                    act.wait_ge(o_turned.sem, o_turned.at(l, 1) + i)
                    for h in range(2):
                        r = slice(64 * h, 64 * h + 64)
                        for smp in range(4):
                            o = PS[r, 5, smp * P:smp * P + P].rearrange("d (p c) -> d p c", p=PR)
                            at_ = 8 * smp + TS * h
                            act.activation(Y[r, 4:8, ds(i * 4 * TS + (NP + TS * smp), TS)], o[:, :, at_:at_ + TS],
                                           ACT.Copy)
                act.drain()
                act.wait_ge(gla_done.sem, gla_done.at(l, 1))
                act.wait_ge(op_evac.sem, op_evac.at(l, PR))
                act.activation(a_hi[:, :, :], Y[:, :, :], ACT.Copy).then_inc(heads_round.sem, 1)

                act.sem_inc(yb_free.sem, 2)
                for j in range(N_MO):
                    if j < 2:
                        split(l, POS_MO, 1, j % 2)
                    elif j == 2:
                        split(l, POS_IN[1], 0, 0)
                    act.wait_ge(w_used.sem, w_used.at(l, POS_MO + j + 1))
                    act.activation(Y[:, 2 * j:2 * j + 2, :], PS[:, 2 * (j % 2):2 * (j % 2) + 2, 0:T], ACT.Copy)
                    act.activation(ysq[:, 2 * (j % 2):2 * (j % 2) + 2, :], PS[:, 2 * (j % 2):2 * (j % 2) + 2, 0:T],
                                   ACT.Square).then_inc(yb_free.sem, 1)
                split(l, POS_IN[1], 0, 1)
                seam_post(l, 1)
                pre(l, 2)
                ffn(l, 1, (l + 1, POS_IN[0]))
                seam_post(l, 2)
            act.wait_ge(out_t.sem, 1)
            for i in range(3):
                n = P if i < PT_ else NS
                last = act.activation(xtok[0:n, i, :], PS[0:n, 2 * i:2 * i + 2, :].rearrange("p a b -> p (a b)"),
                                      ACT.Copy)
            last.then_inc(out_copied.sem, 1)

        @block.vector
        def _(dve):
            tt, ts_, stt, cp = dve.tensor_tensor, dve.tensor_scalar, dve.scalar_tensor_tensor, dve.tensor_copy

            def split(l, pos, i, s, kind="in"):
                for h, (at_, n) in enumerate(halves(kind)):
                    dve.wait_ge(hi_done.sem, hi_done.at(l, 2 * (pos + s) + h + 1) + 4 * i)
                    tt(w_lo[:, s, at_:at_ + n], raw[:, s, at_:at_ + n], w_hi[:, s, at_:at_ + n],
                       ALU.subtract).then_inc(lo_done.sem, 1)

            def copy_sums(used, i, pair):
                dve.wait_ge(direct_used.sem, used + 2 * pair + 2 + 4 * i)
                cp(crow[:, ds(i * 2 * P + pair * P, P)], PS[:, 6 + pair, 0:P]).then_inc(cond_copied.sem, 1)

            def modulation(i, v):
                m = M[:, i, :, :]
                acc = PS[:, 6:8, :].rearrange("p a (k c) -> p (a k) c", c=32)[:, 0:NF, 0:NC]

                def col(a, n):
                    return v(a, n).unsqueeze(2).to_broadcast([P, n, NC])
                tt(m, acc, col(V_CB + NF * i, NF), ALU.add)
                dve.drain()
                stt(m[:, KB:2 * KB, :], m[:, KB:2 * KB, :], 1.0, col(V_PRE + KB * i, KB), ALU.add, ALU.mult)
                stt(m[:, 2 * KB:, :], m[:, 2 * KB:, :], 1.0 if i == 1 else 0.5, col(V_POST + KB * i, KB),
                    ALU.mult, ALU.mult).then_inc(mod_ready.sem, 1)

            def sample(t, k0=0, k1=KB):
                return t[:, k0:k1, NP:T].rearrange("p k (b t) -> p k b t", t=TS)

            def per_sample(i, k0):
                return M[:, i, k0:k0 + KB, 1:NC].unsqueeze(3).to_broadcast([P, KB, B, TS])

            def over_blocks(row, n=KB):
                return row.unsqueeze(1).to_broadcast([P, n, T])

            def gate_prompt(k, kb0, kb1):
                for kb in range(kb0, kb1):
                    ts_(Y[:, kb, 0:NP], Y[:, kb, 0:NP], M[:, k, 2 * KB + kb, 0:1], None, ALU.mult)

            def scale_samples(p):
                tt(sample(Y), sample(X), per_sample(p, KB), ALU.mult)

            def seam_post(l, k, yb, gated, after):
                dve.wait_ge(yb_free.sem, yb_free.at(l, yb))
                gate_prompt(k, gated, KB)
                tt(sample(Y), sample(Y), per_sample(k, 2 * KB), ALU.mult)
                dve.drain()
                dve.wait_ge(std_y.sem, std_y.at(l, k + 1))
                for j in range(KP):
                    y, x = Y[:, 2 * j:2 * j + 2, :], X[:, 2 * j:2 * j + 2, :]
                    tt(y, y, over_blocks(rstd[:, 0, :], 2), ALU.mult)
                    dve.drain()
                    tt(x, x, y, ALU.add).then_inc(x_upd.sem, 1)
                dve.drain()
                scale_samples((k + 1) % 3)
                split(*after, 0, 1)

            def pre(l, p):
                dve.drain()
                dve.wait_ge(x_scaled.sem, x_scaled.at(l, p))
                dve.wait_ge(std_x.sem, std_x.at(l, p + 1))

                def low(j):
                    dve.wait_ge(a_round.sem, a_round.at(l, p * KP + j + 1))
                    for kb in (2 * j, 2 * j + 1):
                        stt(a_lo[:, kb, 0:NP], Y[:, kb, 0:NP], M[:, p, kb, 0:1], a_hi[:, kb, 0:NP],
                            ALU.add, ALU.subtract)
                    tt(a_lo[:, 2 * j:2 * j + 2, NP:T], Y[:, 2 * j:2 * j + 2, NP:T],
                       a_hi[:, 2 * j:2 * j + 2, NP:T], ALU.subtract).then_inc(a_ready.sem, 1)

                for j in range(KP):
                    y = Y[:, 2 * j:2 * j + 2, :]
                    tt(y, y, over_blocks(rstd[:, 1, :], 2), ALU.mult)
                    dve.drain()
                    tt(sample(Y, 2 * j, 2 * j + 2), sample(Y, 2 * j, 2 * j + 2),
                       M[:, p, 2 * j:2 * j + 2, 1:NC].unsqueeze(3).to_broadcast([P, 2, B, TS]), ALU.add)\
                        .then_inc(a_f32.sem, 1)
                    if j:
                        low(j - 1)
                low(KP - 1)

            def ffn(l, n, after):
                pos, out = POS_IN[n], POS_OUT[n]
                dve.sem_inc(gu_free.sem, 2)

                def hidden(j, s):
                    dve.wait_ge(silu_done.sem, silu_done.at(l, n * N_IN + 1) + j)
                    at_ = slice(j, j + 1) if isinstance(j, int) else ds(j, 1)
                    tt(hf[:, s:s + 1, :], sg[:, s:s + 1, :], PS[:, 2 + s:3 + s, 0:T], ALU.mult)\
                        .then_inc(gu_free.sem, 1)
                    dve.drain()
                    cp(h_hi[:, at_, :], hf[:, s:s + 1, :])
                    dve.drain()
                    tt(h_lo[:, at_, :], hf[:, s:s + 1, :], h_hi[:, at_, :], ALU.subtract)\
                        .then_inc(h_ready.sem, 1)

                i_in = 1 if n == 0 else 0
                with dve.Fori(0, NCH // 4) as i:
                    for s in range(4):
                        split(l, pos, i * 2 + (s // 2 + 1), s % 2)
                        hidden(i * 4 + s, s % 2)
                        if s >= 2:
                            copy_sums(direct_used.at(l, DP_C[i_in]), i, s - 2)
                with dve.Fori(NCH // 2, N_IN // 2 - 1) as i:
                    for s in range(2):
                        split(l, pos, i + 1, s)
                        hidden(i * 2 + s, s)
                for s in range(2):
                    split(l, out, 0, s, "out")
                    hidden(N_IN - 2 + s, s)
                dve.wait_ge(cond_t.sem, cond_t.at(l, 1 if n == 0 else 3))
                modulation(i_in, (lambda a, k: vec[:, a:a + k]) if n == 0 else (lambda a, k: vecs[:, L - 1, a:a + k]))
                with dve.Fori(0, KB // 2 - 1) as i:
                    for g in range(2):
                        for s in range(2):
                            split(l, out, 2 * i + 1 + g, s, "out")
                        if n == 0:
                            copy_sums(direct_used.at(l, DP_C[2]), i, g)
                for s in range(2):
                    split(l, out, KB - 1, s, "out")
                dve.wait_ge(yb_free.sem, yb_free.at(l, YB_OUT[n] + 2 + KB - 2))
                gate_prompt(2 * n, 0, KB - 2)
                split(*after, 0, 0)
                if n == 0:
                    dve.wait_ge(cond_t.sem, cond_t.at(l, 2))
                    modulation(2, lambda a, k: vec[:, a:a + k])

            dve.sem_inc(lo_done.sem, 4)
            dve.sem_inc(w_used.sem, 2)
            dve.sem_inc(direct_used.sem, 4)
            dve.sem_inc(cond_copied.sem, 2)
            dve.wait_ge(tposed.sem, 1)
            for i in range(3):
                n = P if i < PT_ else NS
                for g in range(2):
                    src = PS[:, 2 + 2 * i + g, :].rearrange("p (k t) -> p k t", k=4)
                    last = cp(X[:, 4 * g:4 * g + 4, P * i:P * i + n], src[:, :, 0:n])
            last.then_inc(start_copied.sem, 1)
            dve.wait_ge(row_set.sem, 1)
            cp(new_mask[:, :, :], PS[:, 2, 0:SG * NS].rearrange("p (g s) -> p g s", g=SG)).then_inc(row_got.sem, 1)
            dve.wait_ge(c_copied.sem, 1)
            for s in range(2):
                split(0, POS_IN[0], 0, s)
            with dve.Fori(0, NCH // 4) as i:
                for pair in range(2):
                    copy_sums(4, i, pair)
            dve.wait_ge(cond_t.sem, 1)
            modulation(0, lambda a, k: vecs[:, 0, a:a + k])
            dve.drain()
            scale_samples(0)

            with dve.Fori(0, L) as l:
                dve.drain()
                cp(vec[:, :].unsqueeze(1), vecs[:, ds(l, 1), :])
                pre(l, 0)
                ffn(l, 0, (l, POS_MI))
                seam_post(l, 0, YB_OUT[0] + 2 + KB, KB - 2, (l, POS_MI))
                pre(l, 1)

                dve.wait_ge(lrw_round.sem, lrw_round.at(l, 1))
                tt(lrw_lo[:, :, 0:LR], lr_raw[:, :, :], lrw_hi[:, :, 0:LR], ALU.subtract)\
                    .then_inc(lrw_ready.sem, 1)
                with dve.Fori(0, N_MI // 2 - 1) as i:
                    for s in range(2):
                        split(l, POS_MI, i + 1, s)
                for s in range(2):
                    split(l, POS_MO, 0, s)

                dve.wait_ge(mix_evac.sem, mix_evac.at(l, N_MI + 2))
                dve.wait_ge(zeroed.sem, zeroed.at(l, 1))
                for h in range(2):
                    r = slice(64 * h, 64 * h + 64)
                    last = cp(qz[r, :, h, :], Fm[r, SQ:SQ + PR, :])
                last.then_inc(qz_ready.sem, 1)
                dve.wait_ge(mean_sum.sem, mean_sum.at(l, 1))
                for j in range(GP):
                    stt(dm[:, j, :], PS[:, 6, 0:T], -1.0 / GW, Fm[:, MV + j, :], ALU.mult, ALU.add)
                dve.drain()
                tt(dsq[:, :, :], dm[:, :, :], dm[:, :, :], ALU.mult).then_inc(dev_ready.sem, 1)

                def values(i):
                    n = P if i < PT_ else NS
                    dve.wait_ge(kv_t.sem, kv_t.at(l, 2 * i + 2))
                    cp(sv[0:n, i, :], PS[0:n, 3, :]).then_inc(kv_v.sem, 1)
                values(0)
                dve.wait_ge(gate_sum.sem, gate_sum.at(l, 1))
                for j in range(GP):
                    ts_(gt[0][:, j, :], PS[:, 4 + j, 0:T], vec[:, V_GB + j:V_GB + j + 1], None, ALU.add)
                dve.drain()
                ts_(gt[2][:, :, :], gt[0][:, :, :], 0.0, None, ALU.min)
                dve.drain()
                stt(gt[1][:, :, :], gt[2][:, :, :], 2.0, gt[0][:, :, :], ALU.mult, ALU.subtract)\
                    .then_inc(gate_n.sem, 1)
                values(1)
                values(2)
                dve.wait_ge(gm_std.sem, gm_std.at(l, 1))
                tt(dm[:, :, :], dm[:, :, :], over_blocks(rstd[:, 0, :], GP), ALU.mult)
                dve.drain()
                for j in range(GP):
                    last = ts_(dm[:, j, :], dm[:, j, :], vec[:, V_LW + j:V_LW + j + 1],
                               vec[:, V_LB + j:V_LB + j + 1], ALU.mult, ALU.add)
                last.then_inc(vn_f.sem, 1)
                dve.wait_ge(gate_l.sem, gate_l.at(l, 1))
                tt(gt[0][:, :, :], gt[2][:, :, :], gt[1][:, :, :], ALU.subtract)
                dve.drain()
                for j in range(GP):
                    dve.tensor_tensor_scan(gt[2][:, j, :], restart[:, :], gt[0][:, j, :], 0.0,
                                           ALU.mult, ALU.add)
                dve.drain()
                for t0, t1, c in ((0, NP, GC), (NP, T, TS)):
                    b_ = gt[2][:, :, t0:t1].rearrange("p j (n c) -> p j n c", c=c)
                    d_ = gt[3][:, :, t0:t1].rearrange("p j (n c) -> p j n c", c=c)
                    last = tt(d_, b_[:, :, :, c - 1:c].to_broadcast([P, GP, (t1 - t0) // c, c]), b_,
                              ALU.subtract)
                last.then_inc(gate_b.sem, 1)
                dve.wait_ge(gate_e.sem, gate_e.at(l, 1))
                dve.wait_ge(zeroed.sem, zeroed.at(l, 2))
                tt(gt[3][:, :, :], gt[3][:, :, :], Fm[:, GK:GK + GP, :], ALU.mult)
                tt(gt[0][:, :, :], gt[0][:, :, :], Fm[:, GK:GK + GP, :], ALU.mult)
                for h in range(2):
                    r = slice(64 * h, 64 * h + 64)
                    last = stt(gqz[r, :, h, :], Fm[r, GQ:GQ + GP, :], HD ** -0.5, gt[1][r, :, :],
                               ALU.mult, ALU.mult)
                last.then_inc(gla_in.sem, 1)

                dve.wait_ge(gm_t.sem, gm_t.at(l, 1))
                tt(wst[:, :, :], PS[:, 3, :].rearrange("p (h t) -> p h t", h=GH),
                   causal[:, :].unsqueeze(1).to_broadcast([P, GH, P]), ALU.mult).then_inc(gm_tc.sem, 1)
                for i in range(3):
                    n = P if i < PT_ else NS
                    dve.wait_ge(gm_t.sem, gm_t.at(l, 2 + i))
                    cp(vn[0:n, i, :], PS[0:n, 1 + i % 2, 0:GW]).then_inc(gm_tc.sem, 1)
                dve.wait_ge(wss_sum.sem, wss_sum.at(l, 1))
                tt(wss[:, :, :].rearrange("s h (b t) -> s h b t", t=TS),
                   PS[0:NS, 4, 0:GH * TS].rearrange("s (h t) -> s h t", h=GH).unsqueeze(2)
                   .to_broadcast([NS, GH, B, TS]),
                   same_s[:, :].unsqueeze(1).unsqueeze(3).to_broadcast([NS, GH, B, TS]), ALU.mult)\
                    .then_inc(wss_ready.sem, 1)
                dve.wait_ge(k_out.sem, k_out.at(l, 1) * 48)
                dve.wait_ge(bs_in.sem, bs_in.at(l, 1) * 64)
                for i in range(3):
                    dve.wait_ge(gs_sum.sem, gs_sum.at(l, 1 + i))
                    for h in range(2):
                        r = slice(64 * h, 64 * h + 64)
                        if i < PT_:
                            g = PS[r, 1 + i, :].rearrange("p (j h t) -> p j h t", j=GP, h=2)[:, :, h, :]
                            tt(Y[r, 2:4, P * i:P * i + P], g, bs[r, :, :], ALU.add)
                        else:
                            g = PS[r, 3, 0:128].rearrange("p (j h b t) -> p j h b t", j=GP, h=2, t=TS)[:, :, h, :, :]
                            tt(sample(Y, 2, 4)[r], g,
                               bs[r, :, 0:TS].unsqueeze(2).to_broadcast([64, GP, B, TS]), ALU.add)
                dve.drain()
                tt(Y[:, 2:4, :], Y[:, 2:4, :], Fm[:, MU:MU + 2, :], ALU.mult).then_inc(gm_done.sem, 1)

                for i in range(3):
                    dve.wait_ge(gla_t.sem, gla_t.at(l, 1 + i))
                    src = PS[:, 6 + i % 2, :]
                    if i < PT_:
                        cp(gv[:, i, :], src[:, 0:GW])
                        cp(kend[0:64, 2 * i, :], src[0:64, GW:2 * GW])
                        last = cp(kend[64:P, 2 * i + 1, :], src[64:P, GW:2 * GW])
                    else:
                        cp(gv[0:NS, i, :], src[0:NS, 0:GW])
                        last = cp(kend[0:NS, CPB, :], src[0:NS, GW:2 * GW])
                    last.then_inc(gla_tc.sem, 1)
                for i in range(3):
                    dve.wait_ge(att_sum.sem, att_sum.at(l, 1 + i))
                    if i < PT_:
                        tt(att[:, i, :, :, :].rearrange("p j h t -> p (j h) t"),
                           PS[:, 4 + i, :].rearrange("p (g t) -> p g t", t=P),
                           gla_mask[:, :].unsqueeze(1).to_broadcast([P, GH, P]), ALU.mult)\
                            .then_inc(att_ready.sem, 1)
                    else:
                        tt(att_s[:, :, :, :].rearrange("p j h t -> p (j h) t"),
                           PS[0:NS, 0, 0:GH * NS].rearrange("p (g t) -> p g t", t=NS),
                           gla_mask_s[:, :].unsqueeze(1).to_broadcast([NS, GH, NS]), ALU.mult)\
                            .then_inc(att_ready.sem, 1)
                for c in range(CPB):
                    dve.drain()
                    dve.wait_ge(s_sum.sem, s_sum.at(l, c + 1))
                    if c == 0:
                        cp(S[:, 0, :, :], PS[:, 6, 0:GP * P].rearrange("p (j v) -> p j v", j=GP))\
                            .then_inc(s_ready.sem, 1)
                    else:
                        for j in range(GP):
                            e_ = GC * c + GC - 1
                            last = stt(S[:, c % 2, j, :], S[:, (c - 1) % 2, j, :], gt[1][:, j, e_:e_ + 1],
                                       PS[:, 6 + c % 2, j * P:j * P + P], ALU.mult, ALU.add)
                        last.then_inc(s_ready.sem, 1)

                def spread(j):
                    tt(vm[:, :, :], gv[0:NS, 2, j * P:j * P + P].unsqueeze(1).to_broadcast([NS, B, P]),
                       same_s[:, :].unsqueeze(2).to_broadcast([NS, B, P]), ALU.mult).then_inc(vm_ready.sem, 1)
                spread(0)
                for i in range(3):
                    dve.wait_ge(o_sum.sem, o_sum.at(l, 1 + i))
                    for h in range(2):
                        r = slice(64 * h, 64 * h + 64)
                        n = P if i < PT_ else NS
                        src = PS[r, 1 + i, 0:4 * n].rearrange("p (j h t) -> p j h t", j=GP, h=2)[:, :, h, :]
                        cp(gt[0][r, :, P * i:P * i + n], src)
                dve.drain()
                tt(gt[2][:, :, :], gt[0][:, :, :], gt[0][:, :, :], ALU.mult).then_inc(o_sq.sem, 1)
                for j in range(GP):
                    dve.wait_ge(ds_sum.sem, ds_sum.at(l, j + 1))
                    if j == 0:
                        dve.wait_ge(s0_in.sem, s0_in.at(l, 1) * 32)
                    e_ = gt[1][:, j, NP + TS - 1:T:TS]
                    tt(S0[:, :, j, :], S0[:, :, j, :], e_.unsqueeze(2).to_broadcast([P, B, HD]), ALU.mult)
                    dve.drain()
                    for h in range(2):
                        r = slice(64 * h, 64 * h + 64)
                        for q in range(2):
                            src = PS[r, 4 + q, :].rearrange("p (b v) -> p b v", b=4)[:, :, 64 * h:64 * h + 64]
                            last = tt(S0[r, 4 * q:4 * q + 4, j, :], S0[r, 4 * q:4 * q + 4, j, :], src, ALU.add)
                    last.then_inc(s0_new.sem, 1)
                    if j == 0:
                        spread(1)
                dve.wait_ge(o_std.sem, o_std.at(l, 1))
                dve.wait_ge(g_silu.sem, g_silu.at(l, 1))
                tt(gt[0][:, :, :], gt[0][:, :, :], gt[2][:, :, :], ALU.mult)
                dve.drain()
                for j in range(GP):
                    last = stt(Y[:, j, :], gt[0][:, j, :], vec[:, V_GN + j:V_GN + j + 1], Fm[:, GG + j, :],
                               ALU.mult, ALU.mult)
                last.then_inc(gla_done.sem, 1)
                dve.drain()

                dve.wait_ge(z_free.sem, z_free.at(l, SG + 1))
                tt(z[:, :, NOLD:], z[:, :, NOLD:], new_mask[:, :, :], ALU.add)
                dve.drain()
                ts_(sm[:, :, :], z[:, :, :], TOP_Z, None, ALU.min).then_inc(sp_n.sem, 1)
                dve.wait_ge(sp_l.sem, sp_l.at(l, 1))
                tt(sm[:, :, :], sm[:, :, :], z[:, :, :], ALU.max)
                dve.drain()
                for g in range(SG):
                    dve.tensor_tensor_scan(sn[:, g, ::-1], ones[:, 0:1].to_broadcast([P, NKEY]), sm[:, g, ::-1],
                                           0.0, ALU.mult, ALU.add)
                dve.drain()
                tt(z[:, :, :], z[:, :, :], sn[:, :, :], ALU.subtract).then_inc(z_less.sem, 1)

                def softplus(k, parts):
                    for a, n in parts:
                        last = ts_(n, a, TOP_Z, None, ALU.min)
                    last.then_inc(sp_n.sem, 1)
                    dve.wait_ge(sp_l.sem, sp_l.at(l, k))
                    for a, n in parts:
                        last = tt(n, n, a, ALU.max)
                    return last

                dve.wait_ge(zp_evac.sem, zp_evac.at(l, PR))
                neg8 = neg_mask[:, :].unsqueeze(1).to_broadcast([P, SBH, P])
                tt(zp0[:, :, 0:P], zp0[:, :, 0:P], neg8, ALU.add)
                tt(zp1[:, :, :], zp1[:, :, :], neg8, ALU.add)
                dve.drain()
                for g in range(2):
                    snf = sn[:, :, :].rearrange("p a b -> p (a b)")
                    z0, z1 = zp0[:, 4 * g:4 * g + 4, :], zp1[:, 4 * g:4 * g + 4, :]
                    f0 = lambda t: t[:, 0:1024].rearrange("p (h q) -> p h q", h=4)
                    f1 = lambda t: t[:, 1024:1536].rearrange("p (h q) -> p h q", h=4)
                    softplus(2 + g, [(z0, f0(snf)), (z1, f1(snf))]).then_inc(sp_ready.sem, 1)
                    dve.wait_ge(c_sum.sem, c_sum.at(l, 1 + g))
                    tt(z0.rearrange("p (a h) q -> p a (h q)", a=2), z0.rearrange("p (a h) q -> p a (h q)", a=2),
                       PS[:, 0:2, :], ALU.subtract)
                    tt(z1.rearrange("p h q -> p (h q)"), z1.rearrange("p h q -> p (h q)"),
                       PS[:, 2, :], ALU.subtract).then_inc(c_sub.sem, 1)
                for p in range(PR):
                    dve.wait_ge(op_sum.sem, op_sum.at(l, p + 1))
                    for h in range(2):
                        r = slice(64 * h, 64 * h + 64)
                        last = cp(Y[r, 4 + p, 0:NP], PS[r, 6 + p % 2, NP * h:NP * h + NP])
                    last.then_inc(op_evac.sem, 1)
                dve.drain()
                dve.wait_ge(heads_round.sem, heads_round.at(l, 1))
                tt(a_lo[:, :, :], Y[:, :, :], a_hi[:, :, :], ALU.subtract).then_inc(heads_ready.sem, 1)

                for s in range(2):
                    split(l, POS_MO, 1, s)
                split(l, POS_IN[1], 0, 0)
                seam_post(l, 1, YB_MO + 2 + N_MO, 0, (l, POS_IN[1]))
                pre(l, 2)
                dve.wait_ge(outs_done.sem, outs_done.at(l, 1))
                ffn(l, 1, (l + 1, POS_IN[0]))
                seam_post(l, 2, YB_OUT[1] + 2 + KB, KB - 2, (l + 1, POS_IN[0]))

        @block.gpsimd
        def _(pool):
            def select(t, src, pattern, op, base, cm, fill):
                pool.drain()
                return pool.affine_select(out=t, in_=src, compare_op=op, fill=fill, base=base,
                                          pattern=pattern, channel_multiplier=cm)

            ge, gt_, ne = ALU.is_ge, ALU.is_gt, ALU.not_equal
            pool.memset(eps[:, :], EPS)
            pool.memset(cT[:, :, :], 0.0)
            pool.memset(ones[:, :], 1.0)
            pool.memset(ident[:, :], 0.0)
            pool.memset(rep[:, :, :], 0.0)
            pool.memset(head_ones[:, :], 0.0)
            pool.memset(neg_mask[:, :], 0.0)
            pool.memset(row_head[:, :, :, :, :], 0.0)
            pool.memset(row_query[:, :, :, :, :, :], 0.0)
            pool.memset(neg_mask_s[:, :], 0.0)
            pool.memset(same_s[:, :], 1.0)
            pool.memset(gla_mask_s[:, :], 1.0)
            pool.memset(restart[:, :], 1.0)
            select(ident[:, :], ident[:, :], [[-1, P]], ne, 0, 1, 1.0)
            select(rep[:, :, :], rep[:, :, :], [[0, B], [-1, TS]], ne, 0, 1, 1.0)
            pool.memset(head_ones[0:64, 0:64], 1.0)
            pool.memset(head_ones[64:P, 64:P], 1.0)
            pool.drain()
            pool.memset(restart[:, 0:NP:GC], 0.0)
            pool.drain()
            pool.memset(restart[:, NP:T:TS], 0.0)
            select(suffix[:, :], ones[:, :], [[-1, P]], ge, 0, 1, 0.0)
            select(causal[:, :], ones[:, :], [[1, P]], ge, 0, -1, 0.0)
            select(gla_mask[:, :], ones[:, :], [[1, P]], ge, 0, -1, 0.0)
            pool.drain()
            pool.memset(gla_mask[0:64, 64:P], 0.0)
            select(neg_mask[:, :], neg_mask[:, :], [[1, P]], gt_, 0, -1, MASKED)
            select(same_s[:, :], same_s[:, :], [[-TS, B]], ge, 0, 1, 0.0)
            select(same_s[:, :], same_s[:, :], [[TS, B]], ge, TS - 1, -1, 0.0)
            for p in range(PR):
                select(row_head[:, p, :, :, :], row_head[:, p, :, :, :], [[0, 4], [-1, 2], [0, TS]], ne, -2 * p, 1, 1.0)
                for g in range(SG):
                    select(row_query[:, g, p, :, :, :], row_query[:, g, p, :, :, :],
                           [[-TS, 4], [0, 2], [-1, TS]], ne, -4 * TS * g, 1, 1.0)
            for t, op, step, fill in ((gla_mask_s, ge, 1, 0.0), (neg_mask_s, gt_, -1, MASKED)):
                select(t[:, :], t[:, :], [[step, NS]], op, 0, -step, fill)
                v = t[:, :].rearrange("s (b t) -> s b t", t=TS)
                select(v, v, [[-TS, B], [0, TS]], ge, 0, 1, fill)
                last = select(v, v, [[TS, B], [0, TS]], ge, TS - 1, -1, fill)
            last.then_inc(const_ready.sem, 1)

            def after(sig, l, k):
                pool.wait_ge(sig.sem, sig.at(l, k))
                pool.sem_inc(pool_past.sem, 1)

            with pool.Fori(0, L) as l:
                after(ssy_done, l, 1)
                lrc = mix_w_in[l, :, LRC:LRC + LR].rearrange("(k p) c -> p k c", p=P)
                pool.dma_start(lr_raw[:, :, :], lrc).then_inc(small_in.sem, 16)
                pool.dma_start(w2[:, :], gla_w_gate2[l, :, :]).then_inc(small_in.sem, 16)
                pool.dma_start(sbb[:, :], sb_bias[l, :].partition_broadcast(P)).then_inc(small_in.sem, 16)
                pool.dma_start(sb_col[:, :], sb_bias[l, :].unsqueeze(1)).then_inc(small_in.sem, 16)
                pool.memset(lrw_hi[:, :, :].bitcast(F32), 0.0)
                pool.memset(lrw_lo[:, :, :].bitcast(F32), 0.0)
                pool.memset(qz[:, :, :, :], 0.0).then_inc(zeroed.sem, 1)
                after(lr_sum, l, 1)
                pool.dma_start(wsr[:, :, :], gm_ws[l, :, :, :].rearrange("h t s -> t h s")).then_inc(ws_in.sem, 16)
                for j in range(GP):
                    for h in range(2):
                        pool.dma_start(bs[64 * h:64 * h + 64, j, :], gm_bs[l, 2 * j + h, :].partition_broadcast(64))\
                            .then_inc(bs_in.sem, 16)
                for j in range(GP):
                    pool.dma_start(S0[:, :, j, :], state_gla[l, :, 2 * j:2 * j + 2, :, :]
                                   .rearrange("b h k v -> (h k) b v")).then_inc(s0_in.sem, 16)
                pool.memset(qd[:, :, :, :], 0.0)
                pool.memset(gqz[:, :, :, :], 0.0)
                pool.memset(kend[:, :, :], 0.0).then_inc(zeroed.sem, 1)
                after(kv_k, l, 3)
                after(kv_v, l, 3)
                for t, pr, sa, done in ((kst, k_prompt, k_sample, k_out), (sv, v_prompt, v_sample, v_out)):
                    for i in range(PT_):
                        pool.dma_start(pr[l, 0, P * i:P * i + P, :, :].rearrange("s h d -> s (h d)"), t[:, i, :])\
                            .then_inc(done.sem, 16)
                    pool.dma_start(sa[l, :, :, :, :].rearrange("b t h d -> (b t) (h d)"), t[0:NS, 2, :])\
                        .then_inc(done.sem, 16)
                after(gm_tc, l, 4)
                pool.dma_start(gm_v_sample[l, :, :, :].rearrange("b t d -> (b t) d"), vn[0:NS, 2, :])\
                    .then_inc(gmv_out.sem, 16)
                after(s_ready, l, CPB)
                for h in range(2):
                    pool.dma_start(s_prompt[l, 0, h::2, :, :].rearrange("j k v -> k j v"),
                                   S[64 * h:64 * h + 64, (CPB - 1) % 2, :, 64 * h:64 * h + 64])\
                        .then_inc(sp_out.sem, 16)
                after(s0_new, l, GP)
                for j in range(GP):
                    pool.dma_start(s_sample[l, :, 2 * j:2 * j + 2, :, :].rearrange("b h k v -> (h k) b v"),
                                   S0[:, :, j, :]).then_inc(ss_out.sem, 16)
                pool.wait_ge(k_out.sem, k_out.at(l, 1) * 48)
                pool.wait_ge(v_out.sem, v_out.at(l, 1) * 48)
                pool.wait_ge(gmv_out.sem, gmv_out.at(l, 1) * 16)
                pool.wait_ge(sp_out.sem, sp_out.at(l, 1) * 32)
                pool.wait_ge(ss_out.sem, ss_out.at(l, 1) * 32)
                pool.sem_inc(outs_done.sem, 1)


INPUTS = ["x_prompt", "x_sample", "c_prompt", "c_sample", "cache_sb_k", "cache_sb_v", "state_gla",
          "page_table", "cond_w", "cond_b", "norm_pre", "norm_post", "ffn_w_in", "ffn_w_out",
          "mix_w_in", "mix_w_out", "gla_w_gate2", "gla_b_gate", "gla_norm", "gm_ln_w", "gm_ln_b",
          "gm_ws", "gm_bs", "sb_bias"]


def kernel(**inputs):
    import concourse.bacc as bacc
    from concourse.bass_utils import run_bass_kernel_spmd

    a = {name: np.ascontiguousarray(inputs[name]) for name in INPUTS}
    depth, _, _, sb_heads, hd = a["cache_sb_k"].shape
    batch, seq, d = a["x_prompt"].shape
    dec, dseq, _ = a["x_sample"].shape
    gh = a["state_gla"].shape[2]
    gm_w = a["gm_ln_w"].shape[1]
    outputs = [(batch, seq, d), (dec, dseq, d), (depth, batch, gh, hd, hd), (depth, dec, gh, hd, hd),
               (depth, batch, seq, sb_heads, hd), (depth, batch, seq, sb_heads, hd),
               (depth, dec, dseq, sb_heads, hd), (depth, dec, dseq, sb_heads, hd),
               (depth, dec, dseq, gm_w)]
    nc = bacc.Bacc("TRN2", target_bir_lowering=False, num_devices=1)
    args = [nc.dram_tensor(f"in_{n}", a[n].shape, mybir.dt.from_np(a[n].dtype), kind="ExternalInput").ap()
            for n in INPUTS]
    args += [nc.dram_tensor(f"out_{i}", s, F32, kind="ExternalOutput").ap() for i, s in enumerate(outputs)]
    decoder_step(nc, *args)
    r = run_bass_kernel_spmd(nc, [{f"in_{n}": a[n] for n in INPUTS}], core_ids=[0])
    return tuple(r.results[0][f"out_{i}"] for i in range(len(outputs)))
```
